# Optimizing a Trainium2 kernel written in Bass

```python
import jax
import jax.numpy as jnp
from jax import lax
import numpy as np

D_MODEL = 1024
BATCH = 1
SEQ = 256
DEPTH = 2

GRID_W = 64
CTX_LEN = 256
CHUNK = 128
ROWS_PER_CHUNK = CHUNK // GRID_W
A_GROUPS = 4
A_DIM = 128
A_WIDTH = A_GROUPS * A_DIM
B_HEADS = 4
B_DIM = 128
B_WIDTH = B_HEADS * B_DIM
MIX_WIDTH = A_WIDTH + B_WIDTH
REC_HEADS = 8
REC_DK = 128
REC_DV = 128
REC_WIDTH = REC_HEADS * REC_DV
SCAN_CHUNK = 64
D_FF = 2816
N_EXPERTS = 8
TOP_K = 2
D_EXPERT = 3584
EPS = 1e-6
F_FLOOR = 1e-30

kernel_name = 'hybrid_fourier_gmlp_hgrn2_moe_dit'

def rmsnorm(x, gain):
    xf = x.astype(jnp.float32)
    y = xf * lax.rsqrt(jnp.mean(xf * xf, axis=-1, keepdims=True) + EPS)
    return (y * gain.astype(jnp.float32)).astype(x.dtype)

def ada_mod(cond, w, b):
    m = jax.nn.silu(cond) @ w + b
    return jnp.split(m[..., None, :], 6, axis=-1)

def modulate(h, shift, scale):
    return h * (1.0 + scale) + shift

def even_mixer(h, w_in, gmlp_w, gmlp_b, w_out, n_chunks):
    bsz, t, _ = h.shape
    p = h @ w_in
    a = p[..., :A_WIDTH].reshape(bsz, t, A_GROUPS, A_DIM)
    uv = jax.nn.gelu(p[..., A_WIDTH:], approximate=False).reshape(bsz, t, 2, B_HEADS, B_DIM)
    u, v = uv[:, :, 0], uv[:, :, 1]
    ya = jnp.real(jnp.fft.fft2(a.astype(jnp.float32), axes=(1, 3), norm='ortho'))
    vf = v.astype(jnp.float32)
    vn = (vf - jnp.mean(vf, axis=-1, keepdims=True)) * lax.rsqrt(jnp.var(vf, axis=-1, keepdims=True) + EPS)
    vn = vn.reshape(bsz, n_chunks, CHUNK, B_HEADS, B_DIM)
    z = jnp.einsum('hts,bnshc->bnthc', gmlp_w.astype(jnp.float32), vn) + gmlp_b.astype(jnp.float32).T[:, :, None]
    yb = u.astype(jnp.float32) * z.reshape(bsz, t, B_HEADS, B_DIM)
    y = jnp.concatenate([ya.reshape(bsz, t, A_WIDTH), yb.reshape(bsz, t, B_WIDTH)], axis=-1)
    return y.astype(h.dtype) @ w_out

def split_heads(a):
    return a.reshape(a.shape[0], a.shape[1], REC_HEADS, -1)

def hgrn_gates(z, lb):
    lb = lb.reshape(REC_HEADS, REC_DK)
    f = lb + (1.0 - lb) * jax.nn.sigmoid(z)
    log_f = jnp.log(jnp.maximum(f, F_FLOOR))
    k = (1.0 - lb) * jax.nn.sigmoid(-z)
    return k, log_f

def rec_query_gate(p):
    q = jax.nn.silu(split_heads(p[..., :REC_WIDTH].astype(jnp.float32))) * REC_DK ** -0.5
    g = p[..., REC_WIDTH:2 * REC_WIDTH]
    return q, g

def rec_state_inputs(p_state, lb_fwd, lb_bwd):
    zf, zb, i = [split_heads(a.astype(jnp.float32)) for a in jnp.split(p_state, 3, axis=-1)]
    return i, hgrn_gates(zf, lb_fwd), hgrn_gates(zb, lb_bwd)

def gla_scan(q, k, v, log_f, s0):
    bsz, t, nh, _ = q.shape
    nc = t // SCAN_CHUNK

    def chunks(a):
        return a.reshape(bsz, nc, SCAN_CHUNK, nh, a.shape[-1]).transpose(1, 0, 3, 2, 4)

    lower = jnp.tril(jnp.ones((SCAN_CHUNK, SCAN_CHUNK), dtype=bool))[:, :, None]

    def step(s, blk):
        qc, kc, vc, gc = blk
        b = jnp.cumsum(gc, axis=2)
        diff = b[:, :, :, None, :] - b[:, :, None, :, :]
        decay = jnp.where(lower, jnp.exp(jnp.where(lower, diff, 0.0)), 0.0)
        scores = jnp.einsum('bhtd,bhsd,bhtsd->bhts', qc, kc, decay)
        o = scores @ vc + jnp.einsum('bhtd,bhde->bhte', qc * jnp.exp(b), s)
        b_end = b[:, :, -1:, :]
        s_new = jnp.exp(b_end[:, :, 0, :, None]) * s + jnp.einsum('bhsd,bhse->bhde', kc * jnp.exp(b_end - b), vc)
        return s_new, o

    s_fin, o = lax.scan(step, s0, (chunks(q), chunks(k), chunks(v), chunks(log_f)))
    return o.transpose(1, 0, 3, 2, 4).reshape(bsz, t, nh, -1), s_fin

def gla_final_state(k, v, log_f):
    b = jnp.cumsum(log_f, axis=1)
    return jnp.einsum('bthd,bthe->bhde', k * jnp.exp(b[:, -1:] - b), v)

def flip(a):
    return jnp.flip(a, axis=1)

def bidir_scan(q, i, fwd, bwd, s_fwd, s_bwd):
    o_f, sf_out = gla_scan(q, fwd[0], i, fwd[1], s_fwd)
    o_b, sb_out = gla_scan(flip(q), flip(bwd[0]), flip(i), flip(bwd[1]), s_bwd)
    return o_f + flip(o_b), sf_out, sb_out

def rec_output(o, g, gain, w_out, dtype):
    bsz, t = o.shape[:2]
    y = rmsnorm(o, gain.reshape(REC_HEADS, REC_DV)) * jax.nn.silu(split_heads(g.astype(jnp.float32)))
    return y.reshape(bsz, t, REC_WIDTH).astype(dtype) @ w_out

def swiglu(h, w1, w3, w2):
    return (jax.nn.silu(h @ w1) * (h @ w3)) @ w2

def moe_swiglu(h, router_w, w1, w3, w2):
    logits = (h @ router_w).astype(jnp.float32)
    top_v, top_i = lax.top_k(logits, TOP_K)
    top_p = jax.nn.softmax(top_v, axis=-1)
    comb = jnp.sum(jax.nn.one_hot(top_i, N_EXPERTS, dtype=jnp.float32) * top_p[..., None], axis=-2).astype(h.dtype)
    y = jnp.zeros_like(h)
    for e in range(N_EXPERTS):
        y = y + comb[..., e:e + 1] * swiglu(h, w1[e], w3[e], w2[e])
    return y

def setup_inputs(seed: int = 0) -> dict:
    key = jax.random.key(seed)
    ks = jax.random.split(key, 24)
    n_even = (DEPTH + 1) // 2
    n_odd = DEPTH // 2

    def nrm(k, shape, scale):
        return jax.random.normal(k, shape, jnp.float32) * scale

    def gain(k, shape, noise=0.02):
        return 1.0 + nrm(k, shape, noise)

    return {
        'x': nrm(ks[0], (BATCH, SEQ, D_MODEL), 1.0),
        'c': nrm(ks[1], (BATCH, D_MODEL), 1.0),
        'ctx': nrm(ks[2], (BATCH, CTX_LEN, D_MODEL), 1.0),
        'c_ctx': nrm(ks[3], (D_MODEL,), 1.0),
        'w_ada': nrm(ks[4], (DEPTH, D_MODEL, 6 * D_MODEL), 0.5 * D_MODEL ** -0.5),
        'b_ada': nrm(ks[5], (DEPTH, 6 * D_MODEL), 0.02),
        'norm_mix': gain(ks[6], (DEPTH, D_MODEL)),
        'norm_ffn': gain(ks[7], (DEPTH, D_MODEL)),
        'norm_out': gain(ks[8], (D_MODEL,)),
        'w_in_even': nrm(ks[9], (n_even, D_MODEL, A_WIDTH + 2 * B_WIDTH), D_MODEL ** -0.5),
        'gmlp_w': nrm(ks[10], (n_even, B_HEADS, CHUNK, CHUNK), 0.5 * CHUNK ** -0.5),
        'gmlp_b': gain(ks[11], (n_even, B_HEADS, CHUNK)),
        'w_out_even': nrm(ks[12], (n_even, MIX_WIDTH, D_MODEL), MIX_WIDTH ** -0.5),
        'w_in_odd': nrm(ks[13], (n_odd, D_MODEL, 5 * REC_WIDTH), D_MODEL ** -0.5),
        'rec_lb': gain(ks[14], (n_odd, 2, REC_WIDTH), 0.1),
        'rec_norm': gain(ks[15], (n_odd, REC_WIDTH)),
        'w_out_odd': nrm(ks[16], (n_odd, REC_WIDTH, D_MODEL), REC_WIDTH ** -0.5),
        'ffn_w1': nrm(ks[17], (n_even, D_MODEL, D_FF), D_MODEL ** -0.5),
        'ffn_w3': nrm(ks[18], (n_even, D_MODEL, D_FF), D_MODEL ** -0.5),
        'ffn_w2': nrm(ks[19], (n_even, D_FF, D_MODEL), D_FF ** -0.5),
        'router_w': nrm(ks[20], (n_odd, D_MODEL, N_EXPERTS), D_MODEL ** -0.5),
        'moe_w1': nrm(ks[21], (n_odd, N_EXPERTS, D_MODEL, D_EXPERT), D_MODEL ** -0.5),
        'moe_w3': nrm(ks[22], (n_odd, N_EXPERTS, D_MODEL, D_EXPERT), D_MODEL ** -0.5),
        'moe_w2': nrm(ks[23], (n_odd, N_EXPERTS, D_EXPERT, D_MODEL), D_EXPERT ** -0.5),
    }

def reference(x, c, ctx, c_ctx, w_ada, b_ada, norm_mix, norm_ffn, norm_out,
              w_in_even, gmlp_w, gmlp_b, w_out_even,
              w_in_odd, rec_lb, rec_norm, w_out_odd,
              ffn_w1, ffn_w3, ffn_w2, router_w, moe_w1, moe_w3, moe_w2):
    bsz, n_lat, _ = x.shape
    rows = n_lat // GRID_W
    lat_chunks = rows // ROWS_PER_CHUNK
    ctx_chunks = ctx.shape[1] // CHUNK
    lb_soft = jax.nn.softmax(rec_lb.astype(jnp.float32), axis=0)
    lower_bounds = jnp.clip(jnp.cumsum(lb_soft, axis=0) - lb_soft[:1], 0.0, 1.0)
    zero_state = jnp.zeros((bsz, REC_HEADS, REC_DK, REC_DV), jnp.float32)
    xc = ctx
    for layer in range(DEPTH):
        last = layer == DEPTH - 1
        j = layer // 2
        sh_m, sc_m, g_m, sh_f, sc_f, g_f = ada_mod(c, w_ada[layer], b_ada[layer])
        sh_mc, sc_mc, g_mc, sh_fc, sc_fc, g_fc = ada_mod(c_ctx, w_ada[layer], b_ada[layer])
        h = modulate(rmsnorm(x, norm_mix[layer]), sh_m, sc_m)
        if layer % 2 == 0:
            y = even_mixer(h, w_in_even[j], gmlp_w[j], gmlp_b[j], w_out_even[j], lat_chunks)
            if not last:
                hc = modulate(rmsnorm(xc, norm_mix[layer]), sh_mc, sc_mc)
                xc = xc + g_mc * even_mixer(hc, w_in_even[j], gmlp_w[j], gmlp_b[j], w_out_even[j], ctx_chunks)
            x = x + g_m * y
        else:
            lb_f, lb_b = lower_bounds[j, 0], lower_bounds[j, 1]
            w_in = w_in_odd[j]
            hc = modulate(rmsnorm(xc, norm_mix[layer]), sh_mc, sc_mc)
            if last:
                ic, fwc, bwc = rec_state_inputs(hc @ w_in[:, 2 * REC_WIDTH:], lb_f, lb_b)
                s_f = gla_final_state(fwc[0], ic, fwc[1])
                s_b = gla_final_state(flip(bwc[0]), flip(ic), flip(bwc[1]))
            else:
                pc = hc @ w_in
                qc, gc = rec_query_gate(pc)
                ic, fwc, bwc = rec_state_inputs(pc[..., 2 * REC_WIDTH:], lb_f, lb_b)
                oc, s_f, s_b = bidir_scan(qc, ic, fwc, bwc, zero_state, zero_state)
                xc = xc + g_mc * rec_output(oc, gc, rec_norm[j], w_out_odd[j], xc.dtype)
            p = h @ w_in
            q, g = rec_query_gate(p)
            i, fw, bw = rec_state_inputs(p[..., 2 * REC_WIDTH:], lb_f, lb_b)
            o, _, _ = bidir_scan(q, i, fw, bw, s_f, s_b)
            x = x + g_m * rec_output(o, g, rec_norm[j], w_out_odd[j], x.dtype)
        hf = modulate(rmsnorm(x, norm_ffn[layer]), sh_f, sc_f)
        if layer % 2 == 0:
            x = x + g_f * swiglu(hf, ffn_w1[j], ffn_w3[j], ffn_w2[j])
            if not last:
                hfc = modulate(rmsnorm(xc, norm_ffn[layer]), sh_fc, sc_fc)
                xc = xc + g_fc * swiglu(hfc, ffn_w1[j], ffn_w3[j], ffn_w2[j])
        else:
            x = x + g_f * moe_swiglu(hf, router_w[j], moe_w1[j], moe_w3[j], moe_w2[j])
            if not last:
                hfc = modulate(rmsnorm(xc, norm_ffn[layer]), sh_fc, sc_fc)
                xc = xc + g_fc * moe_swiglu(hfc, router_w[j], moe_w1[j], moe_w3[j], moe_w2[j])
    return rmsnorm(x, norm_out)


_drawn_inputs = setup_inputs


def setup_inputs(seed=0):
    import zlib

    import numpy as np

    out = dict(_drawn_inputs(seed))
    spreads = {}
    factors = {'ctx': 8.0,
     'c_ctx': 8.0,
     'norm_mix': 6.547,
     'norm_ffn': 10.754,
     'norm_out': 9.193,
     'gmlp_b': 6.526,
     'rec_norm': 25.106}
    for name, (base, spread) in spreads.items():
        noise = np.random.default_rng([zlib.crc32(name.encode()), seed]).standard_normal(out[name].shape)
        drawn = base * np.exp(spread * noise) if base else spread * noise
        out[name] = jnp.asarray(drawn.astype(out[name].dtype))
    for name, factor in factors.items():
        out[name] = (out[name] * factor).astype(out[name].dtype)
    return out
```

```python
from contextlib import ExitStack

import numpy as np

import concourse.bass as bass
from concourse import mybir

F32 = mybir.dt.float32
F32R = mybir.dt.float32r
U8 = mybir.dt.uint8
U32 = mybir.dt.uint32
I32 = mybir.dt.int32
ALU = mybir.AluOpType
ACT = mybir.ActivationFunctionType
AX = mybir.AxisListType

P = 128
D = 1024
KT = D // P
N_LAT = 256
N_CTX = 256
NT = N_LAT + N_CTX
TT = NT // P
LT = N_LAT // P
A_G = 4
B_H = 4
HEADS = 8
HG = 4
R_W = HEADS * P
D_FF = 2816
N_EXP = 8
D_EXP = 3584
EPS = 1e-6
F_FLOOR = 1e-30
Z_MIN = -87.0
LN_CUT = 60
BANK = 512

UNIT = 1024
R = 6
LEAD = 5

FF_COLS = 256
FF_IT = D_FF // FF_COLS
FF_HALF = [(0, 6), (6, FF_IT - 6)]
CB = D_EXP // BANK
EXP_KT = D_EXP // P
UP_UNITS = CB * 8
EXP_UNITS = UP_UNITS + EXP_KT

U_ADA_A = 0
U_IN_EVEN = U_ADA_A + 16
U_ADA_C = U_IN_EVEN + 12
U_OUT_EVEN = U_ADA_C + 8
U_ADA_E = U_OUT_EVEN + 8
U_FFN = U_ADA_E + 24
U_ADA_G = U_FFN + FF_IT * 6
U_IN_ODD = U_ADA_G + 48
U_OUT_ODD = U_IN_ODD + 40
U_MOE = U_OUT_ODD + 8

C_ID, C_ONE, C_IOTA, C_TRI, C_SEL = 0, 128, 256, 384, 512
C_RES = 514
DFT_CS, DFT_CT, DFT_ST = 0, 256, 768
C_DFT = 1280
LEVELS = [64, 32, 16, 8, 4, 2, 1]
C_MASK = len(LEVELS) * 2 * P

V_C, V_CC, V_NMIX, V_NFFN, V_NOUT, V_LB, V_RNORM, V_ROWS = 0, 8, 16, 32, 48, 56, 72, 80
SH_M, SC_M, G_M, SH_F, SC_F, G_F = range(6)

ARENA = 14336
X_ROWS = 0
M_A, M_U, M_V, M_ACS, M_GW, M_DFT, M_TMP = 0, 2048, 4096, 6144, 10240, 10752, 12032
MASK_F = 4096
VEC_ROWS, B_ROWS = 12544, 12672
ADA_ROW = 13312
NORM_AT = [6144, 8192, 8192, 8192, 8192]
F_HID, F_SIL = 0, 6144
E4 = HG * 256
R_KF, R_LF, R_KB, R_LB, R_V, R_T, R_Q, R_G = (E4 * k for k in (0, 2, 4, 6, 8, 10, 12, 13))
X_ACC, X_HID, X_SIL, X_Y, X_OUT = 0, 2048, 2560, 3072, 4096
SLOTS = 128
N_OVER = 2 * N_LAT // (SLOTS + 1)
TURNS = N_EXP + N_OVER
T_TURNS, T_OVER, T_EXPERT = 0, 1, 2
O_SEL, O_ORDER, O_PICK, O_TMP = 0, 8, 16, 16 + 8 * N_OVER


def constants():
    i = np.arange(P)
    c = np.zeros((P, C_RES + C_DFT), np.float32)
    c[:, C_ID:C_ID + P] = np.eye(P)
    c[:, C_ONE:C_ONE + P] = 1.0
    c[:, C_IOTA:C_IOTA + P] = i[None, :]
    c[:, C_TRI:C_TRI + P] = i[:, None] < i[None, :]
    c[[0, 2], C_SEL] = 1.0
    c[[1, 3], C_SEL + 1] = 1.0
    d = c[:, C_RES:]
    w = 2 * np.pi / P * ((i[:, None] * i[None, :]) % P)
    scale = 1.0 / np.sqrt(N_LAT * P)
    d[:, DFT_CS:DFT_CS + P] = np.cos(w) * scale
    d[:, DFT_CS + P:DFT_CS + 2 * P] = np.sin(w) * scale
    t = np.arange(N_LAT)
    w = 2 * np.pi / N_LAT * ((t[:, None] * t[None, :]) % N_LAT)
    for tt in range(LT):
        d[:, DFT_CT + tt * N_LAT:DFT_CT + (tt + 1) * N_LAT] = np.cos(w[tt * P:(tt + 1) * P])
        d[:, DFT_ST + tt * N_LAT:DFT_ST + (tt + 1) * N_LAT] = -np.sin(w[tt * P:(tt + 1) * P])
    m = np.zeros((P, len(LEVELS), 2, P), np.float32)
    for n, h in enumerate(LEVELS):
        block, side = i // (2 * h), i // h % 2
        fwd = (block[:, None] == block[None, :]) & (side[:, None] == 0) & (side[None, :] == 1)
        m[:, n, 0], m[:, n, 1] = fwd, fwd.T
    return c, m.reshape(P, -1)


def build(nc, x, c, ctx_in, c_ctx, w_ada, b_ada, norm_mix, norm_ffn, norm_out, w_in_even, gmlp_wt, gmlp_b,
          w_out_even, w_in_odd, rec_lb, rec_norm, w_out_odd, ffn_w1, ffn_w3, ffn_w2, router_w,
          moe_w1, moe_w3, moe_w2, cst, msk, out):
    es = ExitStack()
    with es:
        def sb(name, shape, dt=F32):
            return es.enter_context(nc.sbuf_tensor(name, shape, dt))

        def sem(name):
            return es.enter_context(nc.semaphore(name))

        raw = sb("raw", [P, R, UNIT])
        w_hi = sb("w_hi", [P, R, UNIT], F32R)
        w_lo = sb("w_lo", [P, R, UNIT], F32R)
        xT = sb("xT", [P, KT, NT])
        h_hi = sb("h_hi", [P, KT * NT], F32R)
        h_lo = sb("h_lo", [P, KT * NT], F32R)
        s_hi = sb("s_hi", [P, 3072], F32R)
        s_lo = sb("s_lo", [P, 3072], F32R)
        arena = sb("arena", [P, ARENA])
        con = sb("con", [P, C_RES])
        masks = sb("masks", [P, C_MASK], U8)
        vT = sb("vT", [P, V_ROWS])
        bT = sb("bT", [P, 96])
        sil = sb("sil", [P, 16])
        cond = sb("cond", [P, KT * 4 + P], F32R)
        adaT = sb("adaT", [P, 2, 48, 2])
        coef = sb("coef", [P, KT, 2])
        stats = sb("stats", [P, 16, 6])
        mv = sb("mv", [P, 16, 2])
        rs = sb("rs", [P, 16])
        lb = sb("lb", [P, 16])
        lb1 = sb("lb1", [P, 16])
        tot = sb("tot", [P, 2, HG, 6])
        rt32 = sb("rt32", [P, KT * N_EXP])
        rt_hi = sb("rt_hi", [P, KT * N_EXP], F32R)
        rt_lo = sb("rt_lo", [P, KT * N_EXP], F32R)
        route = sb("route", [P, LT, 64])
        idx = sb("idx", [P, LT, 8], U32)
        rank = sb("rank", [P, LT, TURNS + 1])
        comb = sb("comb", [P, LT, TURNS + 1])
        trips = sb("trips", [P, T_EXPERT + N_OVER], I32)
        cnt = sb("cnt", [P, T_EXPERT + N_OVER])
        over = sb("over", [P, O_TMP + LT * N_OVER * N_EXP])
        onehot = sb("onehot", [P, LT, SLOTS], F32R)
        spread = sb("spread", [P, N_LAT], F32R)
        cw = sb("cw", [P, LT])
        cslot = sb("cslot", [P, 1])
        y_hi = sb("y_hi", [P, BANK], F32R)
        y_lo = sb("y_lo", [P, BANK], F32R)
        ps = es.enter_context(nc.psum_tensor("ps", [P, 8, BANK], F32))

        ident = con[:, C_ID:C_ID + P]
        ones = con[:, C_ONE:C_ONE + P]
        iota = con[:, C_IOTA:C_IOTA + P]
        tri = con[:, C_TRI:C_TRI + P]

        def ar(at, n):
            return arena[:, at:at + n]

        gb_row = arena[32:33, ADA_ROW:ADA_ROW + B_H * P]

        def hh(kt, a=0, b=NT):
            return h_hi[:, kt * NT + a:kt * NT + b]

        def hl(kt, a=0, b=NT):
            return h_lo[:, kt * NT + a:kt * NT + b]

        def y_parts(half):
            at = EXP_KT * P
            return ((h_hi[:, at:at + BANK], h_lo[:, at:at + BANK]), (y_hi[:, :], y_lo[:, :]))[half]

        raw_in = [sem(f"raw_in{k}") for k in range(R)]
        hi_done, lo_done, pe_used = sem("hi_done"), sem("lo_done"), sem("pe_used")
        vec_in, con_in, x_in, mix_in, rt_in = sem("vec_in"), sem("con_in"), sem("x_in"), sem("mix_in"), sem("rt_in")
        mask_in, mask_rdy = sem("mask_in"), sem("mask_rdy")
        vec_tr, vec_out, x_tr, x_out = sem("vec_tr"), sem("vec_out"), sem("x_tr"), sem("x_out")
        silu_c, cond_hi, cond_rdy, dve_seq = sem("silu_c"), sem("cond_hi"), sem("cond_rdy"), sem("dve_seq")
        lb_dif, lb_exp = sem("lb_dif"), sem("lb_exp")
        ada_row, ada_sel, ada_done = sem("ada_row"), sem("ada_sel"), sem("ada_done")
        sq_done, sq_mm, var_done, std_done = sem("sq_done"), sem("sq_mm"), sem("var_done"), sem("std_done")
        h32_done, hhi_done, h_done = sem("h32_done"), sem("hhi_done"), sem("h_done")
        a_out, u_out, v_out = sem("a_out"), sem("u_out"), sem("v_out")
        lnv, lns, ln_done = sem("lnv"), sem("lns"), sem("ln_done")
        dft_mm, dft_out, y_mm = sem("dft_mm"), sem("dft_out"), sem("y_mm")
        y32_done, yhi_done, ylo_done = sem("y32_done"), sem("yhi_done"), sem("ylo_done")
        resid = sem("resid")
        up_silu, hid_done = sem("up_silu"), sem("hid_done")
        hidhi, hidlo = sem("hidhi"), sem("hidlo")
        z_clip, z_exp, f_rdy, ln_rdy, gates = (sem("z_clip"), sem("z_exp"), sem("f_rdy"), sem("ln_rdy"),
                                              sem("gates"))
        v_rdy, q_rdy, g_rdy = sem("v_rdy"), sem("q_rdy"), sem("g_rdy")
        c_exp, c_mul, c_tr, c_cp, st_mm, st_cp = (sem("c_exp"), sem("c_mul"), sem("c_tr"), sem("c_cp"),
                                                  sem("st_mm"), sem("st_cp"))
        dg_mm, dg_out = sem("dg_mm"), sem("dg_out")
        x_exp, x_mul, x_mm, x_cp = sem("x_exp"), sem("x_mul"), sem("x_mm"), sem("x_cp")
        l_sub, l_exp, l_mul, l_mm, l_cp = sem("l_sub"), sem("l_exp"), sem("l_mul"), sem("l_mm"), sem("l_cp")
        i_exp, i_mul, o_mm, o_cp, o_sq, o_sum = (sem("i_exp"), sem("i_mul"), sem("o_mm"), sem("o_cp"),
                                                 sem("o_sq"), sem("o_sum"))
        o_var, o_std, r32_done, rhi_done, rlo_done = (sem("o_var"), sem("o_std"), sem("r32_done"),
                                                      sem("rhi_done"), sem("rlo_done"))
        rt_hid, rt_rdy, lg_mm, tk_mm, tk_out = (sem("rt_hid"), sem("rt_rdy"), sem("lg_mm"), sem("tk_mm"),
                                                sem("tk_out"))
        rt_dif, rt_exp, pick, rk_mm, routed = sem("rt_dif"), sem("rt_exp"), sem("pick"), sem("rk_mm"), sem("routed")
        acc_rdy, oh_rdy, ga_mm, ga_hi, ga_lo = (sem("acc_rdy"), sem("oh_rdy"), sem("ga_mm"), sem("ga_hi"),
                                                sem("ga_lo"))
        sp_mm, sp_rdy = sem("sp_mm"), sem("sp_rdy")
        eu_silu, eu_hid, et_mm, et_hi, et_lo = (sem("eu_silu"), sem("eu_hid"), sem("et_mm"), sem("et_hi"),
                                                sem("et_lo"))
        ey32, ey_hi, ey_lo, sc_mm = sem("ey32"), sem("ey_hi"), sem("ey_lo"), sem("sc_mm")
        fin32, fin_tr, fin_out, stored = sem("fin32"), sem("fin_tr"), sem("fin_out"), sem("stored")

        block = es.enter_context(nc.Block())

        def slot(u):
            return u % R

        def fills(u):
            return u // R + 1

        def sel_bank(n, bank):
            return (2, 4)[n % 2] if bank == 0 else 6 + n % 2

        def heads(at, a=0, b=NT):
            return ar(at, HG * NT).rearrange("p (h t) -> p h t", h=HG)[:, :, a:b]

        def lat4(at):
            return ar(at, E4).rearrange("p (h t) -> p h t", h=HG)

        @block.sync
        def _(sp):
            def load(u, src, plus=0, reps=0):
                if reps or u >= R:
                    sp.wait_ge(lo_done, plus + (u - R + 1))
                sp.dma_start(raw[:, slot(u), :], src).then_inc(raw_in[slot(u)], 16)

            def cols(w, kt, n, col, width):
                return w[kt * P:(kt + n) * P, col:col + width].rearrange("(k p) c -> p k c", p=P)

            def load_cols(u, w, col, plus=0, reps=0):
                for k in range(4):
                    load(u + k, cols(w, 2 * k, 2, col, BANK), plus, reps)

            vr = ar(VEC_ROWS, P)
            for row, n, v in ((V_C, 8, c[0]), (V_CC, 8, c_ctx), (V_NMIX, 16, norm_mix), (V_NFFN, 16, norm_ffn),
                              (V_NOUT, 8, norm_out), (V_LB, 16, rec_lb[0]), (V_RNORM, 8, rec_norm[0])):
                flat = v if len(v.shape) == 1 else v.rearrange("a b -> (a b)")
                sp.dma_start(vr[row:row + n, :], flat.rearrange("(r q) -> r q", q=P)).then_inc(vec_in, 16)
            sp.dma_start(ar(B_ROWS, P)[0:96, :], b_ada.rearrange("l (r q) -> (l r) q", q=P)).then_inc(vec_in, 16)
            sp.dma_start(con[:, :], cst[:, 0:C_RES]).then_inc(con_in, 16)
            load_cols(U_ADA_A, w_ada[0], 0)
            for s, src in enumerate((x, ctx_in)):
                for t in range(LT):
                    sp.dma_start(ar(X_ROWS + (s * LT + t) * D, D), src[0, t * P:(t + 1) * P, :]).then_inc(x_in, 16)
            for b in range(1, 4):
                load_cols(U_ADA_A + 4 * b, w_ada[0], b * BANK)
            sp.dma_start(ar(MASK_F, C_MASK), msk).then_inc(mask_in, 16)
            sp.dma_start(ar(M_DFT, C_DFT), cst[:, C_RES:]).then_inc(mix_in, 16)
            sp.dma_start(ar(M_GW, B_H * P), gmlp_wt.rearrange("s h t -> s (h t)")).then_inc(mix_in, 16)
            sp.dma_start(gb_row, gmlp_b[0].rearrange("(a h) t -> a (h t)", a=1)).then_inc(mix_in, 16)
            for b in range(3):
                load_cols(U_IN_EVEN + 4 * b, w_in_even[0], b * BANK)
            for b in range(2):
                load_cols(U_ADA_C + 4 * b, w_ada[0], (4 + b) * BANK)
            for b in range(2):
                load_cols(U_OUT_EVEN + 4 * b, w_out_even[0], b * BANK)
            with sp.Fori(0, 2) as j:
                for b in range(3):
                    src = w_ada[0][:, bass.ds(j * (3 * BANK) + (6 + b) * BANK, BANK)]
                    for k in range(4):
                        load(U_ADA_E + 4 * b + k, src[2 * k * P:(2 * k + 2) * P, :].rearrange("(k p) c -> p k c", p=P),
                             plus=j * 12, reps=1)
            u = U_FFN
            for first, n in FF_HALF:
                for it in range(first, first + n):
                    for w in (ffn_w1[0], ffn_w3[0]):
                        for k in range(2):
                            load(u, cols(w, 4 * k, 4, it * FF_COLS, FF_COLS))
                            u += 1
                for ft in range(2 * first, 2 * (first + n)):
                    load(u, ffn_w2[0][ft * P:(ft + 1) * P, :])
                    u += 1
            with sp.Fori(0, 4) as j:
                for b in range(3):
                    src = w_ada[1][:, bass.ds(j * (3 * BANK) + b * BANK, BANK)]
                    for k in range(4):
                        load(U_ADA_G + 4 * b + k, src[2 * k * P:(2 * k + 2) * P, :].rearrange("(k p) c -> p k c", p=P),
                             plus=j * 12, reps=1)
            sp.dma_start(rt32[:, :].rearrange("p (k e) -> p k e", e=N_EXP),
                         router_w[0].rearrange("(k p) e -> p k e", p=P)).then_inc(rt_in, 16)
            u = U_IN_ODD
            for hg in range(2):
                for part in (2, 3, 4, 0, 1):
                    load_cols(u, w_in_odd[0], part * R_W + hg * BANK)
                    u += 4
            for b in range(2):
                load_cols(U_OUT_ODD + 4 * b, w_out_odd[0], b * BANK)

            def expert_loads(e, past):
                def rows(w, kt, n):
                    m = w[0, bass.ds(e, 1), kt * P:(kt + n) * P, :]
                    return m.rearrange("a (k p) c -> p (a k) c", p=P)

                v = 0
                for cb in range(CB):
                    for w in (moe_w1, moe_w3):
                        for k in range(4):
                            load(U_MOE + v, rows(w, 2 * k, 2)[:, :, cb * BANK:(cb + 1) * BANK], past, 1)
                            v += 1
                for kt in range(EXP_KT):
                    load(U_MOE + v, rows(moe_w2, kt, 1), past, 1)
                    v += 1

            with sp.Fori(0, N_EXP) as e:
                expert_loads(e, e * EXP_UNITS)
            sp.wait_ge(routed, 1)
            n_over = sp.value_load(trips[0:1, T_OVER:T_OVER + 1], min_val=0, max_val=N_OVER)
            n_past = sp.value_load(trips[0:1, 0:1], min_val=N_EXP, max_val=TURNS)
            with sp.If(n_over):
                with sp.Fori(0, n_over) as j:
                    e = sp.value_load(trips[0:1, bass.ds(j + T_EXPERT, 1)], min_val=0, max_val=N_EXP - 1)
                    expert_loads(e, j * EXP_UNITS + N_EXP * EXP_UNITS)
                sp.nop()
            for k in range(LEAD):
                load(U_MOE + k, cols(moe_w1[0, 0], 2 * (k % 4), 2, 0, BANK), n_past * EXP_UNITS, 1)

            for t in range(LT):
                sp.wait_ge(fin_out, t + 1)
                sp.dma_start(out[0, t * P:(t + 1) * P, :], ar(X_OUT + t * D, D)).then_inc(stored, 16)
            sp.wait_ge(stored, 16 * LT)

        @block.tensor
        def _(pe):
            def three(dst, s_h, s_l, m_h, m_l, start, stop, **kw):
                pe.matmul(dst, s_h, m_h, start=start, stop=False, **kw)
                pe.matmul(dst, s_l, m_h, start=False, stop=False, **kw)
                return pe.matmul(dst, s_h, m_l, start=False, stop=stop, **kw)

            def unit(u, plus=0):
                pe.wait_ge(lo_done, plus + (u + 1))
                return w_hi[:, slot(u), :], w_lo[:, slot(u), :]

            def ada_sel_mm(n, bank, after):
                pe.wait_ge(ada_row, after + 1)
                if not isinstance(after, int):
                    pe.wait_ge(ada_done, after)
                elif after >= 2:
                    pe.wait_ge(ada_done, after - 1)
                for q in range(4):
                    m = pe.matmul(ps[:, sel_bank(n, bank), 2 * q:2 * q + 2],
                                  ar(ADA_ROW + n % 2 * BANK, BANK)[0:4, q * P:(q + 1) * P],
                                  con[0:4, C_SEL:C_SEL + 2], start=True, stop=True)
                m.then_inc(ada_sel, 1)

            def ada_block(n, u, bank, plus=0):
                b = n % 2
                for k in range(4):
                    hi, lo = unit(u + k, plus)
                    for kk in range(2):
                        kt = 2 * k + kk
                        st = cond[:, kt * 4:kt * 4 + P]
                        pe.matmul(ps[:, bank + b, :], st, hi[:, kk * BANK:(kk + 1) * BANK],
                                  start=(kt == 0), stop=False)
                        m = pe.matmul(ps[:, bank + b, :], st, lo[:, kk * BANK:(kk + 1) * BANK],
                                      start=False, stop=(kt == KT - 1))
                    m.then_inc(pe_used, 1)

            def ada_blocks(n0, count, u, bank):
                for n in range(n0, n0 + count):
                    if n - n0 >= 2:
                        pe.wait_ge(ada_row, n - 1)
                    ada_block(n, u + 4 * (n - n0), bank)
                    if n > n0:
                        ada_sel_mm(n - 1, bank, n - 1)
                ada_sel_mm(n0 + count - 1, bank, n0 + count - 1)

            def norm_sum(n, width):
                for kt in range(KT):
                    pe.wait_ge(sq_done, KT * n + kt + 1)
                    pe.matmul(ps[:, 3, 0:width], ones, ar(NORM_AT[n] + kt % 2 * NT, width),
                              start=(kt == 0), stop=(kt == KT - 1)).then_inc(sq_mm, 1)

            pe.wait_ge(con_in, 16)
            pe.wait_ge(vec_in, 16 * 8)
            pe.transpose(ps[:, 0, 0:V_ROWS], ar(VEC_ROWS, P)[0:V_ROWS, :], con[0:V_ROWS, C_ID:C_ID + V_ROWS])
            pe.transpose(ps[:, 0, 128:224], ar(B_ROWS, P)[0:96, :], con[0:96, C_ID:C_ID + 96]).then_inc(vec_tr, 1)
            pe.wait_ge(x_in, 16 * TT)
            for kt in range(KT):
                if kt == KT - 1:
                    pe.wait_ge(vec_out, 2)
                for t in range(TT):
                    m = pe.transpose(ps[:, (1 + kt) % 8, t * P:(t + 1) * P],
                                     ar(X_ROWS + t * D + kt * P, P), ident)
                m.then_inc(x_tr, 1)

            pe.wait_ge(cond_rdy, 1)
            pe.wait_ge(x_out, 8)
            ada_blocks(0, 4, U_ADA_A, 0)
            norm_sum(0, NT)

            u = U_IN_EVEN
            pe.wait_ge(ada_done, 4)
            for blk, bank in ((0, 0), (1, 4)):
                for k in range(4):
                    hi, lo = unit(u)
                    for kk in range(2):
                        kt = 2 * k + kk
                        if blk == 0:
                            pe.wait_ge(h_done, kt + 1)
                        for n in range(4):
                            a, b = kk * BANK + n * P, kk * BANK + (n + 1) * P
                            m = three(ps[:, bank + n, :], hi[:, a:b], lo[:, a:b], hh(kt), hl(kt), kt == 0, kt == KT - 1)
                    m.then_inc(pe_used, 1)
                    u += 1
            pe.wait_ge(a_out, 4)
            for k in range(4):
                hi, lo = unit(u)
                for kk in range(2):
                    kt = 2 * k + kk
                    for t in range(TT):
                        a, b = t * P, (t + 1) * P
                        m = three(ps[:, t, :], hh(kt, a, b), hl(kt, a, b), hi[:, kk * BANK:(kk + 1) * BANK],
                                  lo[:, kk * BANK:(kk + 1) * BANK], kt == 0, kt == KT - 1)
                m.then_inc(pe_used, 1)
                u += 1

            pe.wait_ge(u_out, 4)
            ada_blocks(4, 2, U_ADA_C, 4)

            pe.wait_ge(mix_in, 48)
            n = 0
            for g in range(A_G):
                for tp in range(2):
                    if n == 0:
                        pe.wait_ge(v_out, 4)
                    if n == 4:
                        pe.wait_ge(ada_done, 6)
                    for q in range(2):
                        t = 2 * tp + q
                        m = pe.matmul(ps[:, n, q * 256:(q + 1) * 256], ar(M_A + g * NT + t * P, P),
                                      ar(M_DFT + DFT_CS, 256), start=True, stop=True)
                    m.then_inc(dft_mm, 1)
                    n += 1
            acs = ar(M_ACS, TT * A_G * 256).rearrange("p (t g c) -> p t g c", t=TT, g=A_G)
            for g in range(A_G):
                pe.wait_ge(dft_out, 2 * (g + 1))
                for s in range(2):
                    for t in range(LT):
                        tok = s * LT + t
                        pe.matmul(ps[:, g, s * 256:(s + 1) * 256], acs[:, tok, g, 0:P],
                                  ar(M_DFT + DFT_CT + t * N_LAT, N_LAT), start=(t == 0), stop=False)
                        m = pe.matmul(ps[:, g, s * 256:(s + 1) * 256], acs[:, tok, g, P:2 * P],
                                      ar(M_DFT + DFT_ST + t * N_LAT, N_LAT), start=False, stop=(t == LT - 1))
                m.then_inc(y_mm, 1)
            pe.wait_ge(dft_out, 8)
            pe.wait_ge(ln_done, 16)
            for h in range(B_H):
                for t in range(TT):
                    m = pe.matmul(ps[:, 4 + h, t * P:(t + 1) * P], ar(M_V + t * BANK + h * P, P),
                                  ar(M_GW + h * P, P), start=(t == 0), stop=False, skip_group_check=True)
                    m = pe.matmul(ps[:, 4 + h, t * P:(t + 1) * P], con[32:33, C_ONE:C_ONE + P],
                                  gb_row[:, h * P:(h + 1) * P], start=False, stop=(t == TT - 1),
                                  skip_group_check=True)
                m.then_inc(y_mm, 1)

            u = U_OUT_EVEN
            for blk in range(2):
                bank = 4 * blk
                for k in range(4):
                    hi, lo = unit(u)
                    for kk in range(2):
                        kt = 2 * k + kk
                        if blk == 0:
                            pe.wait_ge(ylo_done, kt + 1 if kt >= 4 else 4)
                        else:
                            pe.wait_ge(ylo_done, 8)
                        for n in range(4):
                            a, b = kk * BANK + n * P, kk * BANK + (n + 1) * P
                            m = three(ps[:, bank + n, :], hi[:, a:b], lo[:, a:b], hh(kt), hl(kt), kt == 0, kt == KT - 1)
                    m.then_inc(pe_used, 1)
                    u += 1

            pe.wait_ge(resid, 8)
            with pe.Fori(0, 2) as j:
                for n in range(3):
                    ada_block(n, U_ADA_E + 4 * n, 0, plus=j * 12)
                    ada_sel_mm(n, 0, j * 3 + 6 + n)
            norm_sum(1, NT)

            u = U_FFN
            for half, (first, count) in enumerate(FF_HALF):
                for it in range(first, first + count):
                    bank = 4 * (it % 2)
                    if it == 0:
                        pe.wait_ge(ada_done, 12)
                    if it == first and half == 1:
                        pe.wait_ge(resid, 16)
                    elif it - first >= 2:
                        pe.wait_ge(hid_done, it - 1)
                    for w in range(2):
                        for k in range(2):
                            hi, lo = unit(u)
                            for kk in range(4):
                                kt = 4 * k + kk
                                if it == 0 and w == 0:
                                    pe.wait_ge(h_done, KT + kt + 1)
                                for n in range(2):
                                    a, b = kk * FF_COLS + n * P, kk * FF_COLS + (n + 1) * P
                                    m = three(ps[:, bank + 2 * w + n, :], hi[:, a:b], lo[:, a:b], hh(kt), hl(kt),
                                              kt == 0, kt == KT - 1)
                            m.then_inc(pe_used, 1)
                            u += 1
                pe.wait_ge(hid_done, first + count)
                for f in range(2 * count):
                    pe.wait_ge(hidlo, 2 * first + f + 1)
                    hi, lo = unit(u)
                    sl = f % 6 * NT
                    for n in range(KT):
                        m = three(ps[:, n, :], hi[:, n * P:(n + 1) * P], lo[:, n * P:(n + 1) * P],
                                  s_hi[:, sl:sl + NT], s_lo[:, sl:sl + NT], f == 0, f == 2 * count - 1)
                    m.then_inc(pe_used, 1)
                    u += 1

            pe.wait_ge(resid, 24)
            with pe.Fori(0, 4) as j:
                for n in range(3):
                    ada_block(n, U_ADA_G + 4 * n, 0, plus=j * 12)
                    ada_sel_mm(n, 0, j * 3 + 12 + n)
            norm_sum(2, NT)

            u = U_IN_ODD
            for hg in range(2):
                if hg == 0:
                    pe.wait_ge(ada_done, 24)
                for d in range(2):
                    if hg == 1:
                        pe.wait_ge(rlo_done, HG)
                    for k in range(4):
                        hi, lo = unit(u)
                        for kk in range(2):
                            kt = 2 * k + kk
                            if hg == 0 and d == 0:
                                pe.wait_ge(h_done, 2 * KT + kt + 1)
                            for n in range(HG):
                                a, b = kk * BANK + n * P, kk * BANK + (n + 1) * P
                                m = three(ps[:, 4 * d + n, :], hi[:, a:b], lo[:, a:b], hh(kt), hl(kt),
                                          kt == 0, kt == KT - 1)
                        m.then_inc(pe_used, 1)
                        u += 1
                pe.wait_ge(z_clip, 2 * hg + 1)
                for k in range(4):
                    hi, lo = unit(u)
                    for kk in range(2):
                        kt = 2 * k + kk
                        for t in range(TT):
                            a, b = t * P, (t + 1) * P
                            m = three(ps[:, t, :], hh(kt, a, b), hl(kt, a, b), hi[:, kk * BANK:(kk + 1) * BANK],
                                      lo[:, kk * BANK:(kk + 1) * BANK], kt == 0, kt == KT - 1)
                    m.then_inc(pe_used, 1)
                    u += 1
                pe.wait_ge(z_clip, 2 * hg + 2)
                for w in range(2):
                    for k in range(4):
                        hi, lo = unit(u)
                        for kk in range(2):
                            kt = 2 * k + kk
                            for n in range(HG):
                                a, b = kk * BANK + n * P, kk * BANK + (n + 1) * P
                                dst = ps[:, 4 + 2 * w + n // 2, n % 2 * 256:n % 2 * 256 + 256]
                                m = three(dst, hi[:, a:b], lo[:, a:b], hh(kt, 0, N_LAT), hl(kt, 0, N_LAT),
                                          kt == 0 and n % 2 == 0, kt == KT - 1 and n % 2 == 1, skip_group_check=True)
                        m.then_inc(pe_used, 1)
                        u += 1

                pe.wait_ge(v_rdy, hg + 1)
                for d in range(2):
                    pe.wait_ge(c_mul, 2 * hg + d + 1)
                    kbuf = heads((R_KF, R_KB)[d], N_LAT, NT)
                    for seg in range(2):
                        for h in range(HG):
                            m = pe.transpose(ps[:, seg, h * P:(h + 1) * P], kbuf[:, h, seg * P:(seg + 1) * P], ident)
                    m.then_inc(c_tr, 1)
                    pe.wait_ge(c_cp, 2 * hg + d + 1)
                    kt_ = ar(R_T, 2 * BANK).rearrange("p (s h c) -> p s h c", s=2, h=HG)
                    for h in range(HG):
                        for seg in range(2):
                            m = pe.matmul(ps[:, 2 + d, h * P:(h + 1) * P], kt_[:, seg, h, :],
                                          ar(R_V + (2 + seg) * BANK + h * P, P), start=(seg == 0), stop=(seg == 1))
                    m.then_inc(st_mm, 1)

                pe.wait_ge(q_rdy, hg + 1)
                pe.wait_ge(g_rdy, hg + 1)
                kf, kb, q4 = heads(R_KF, 0, N_LAT), heads(R_KB, 0, N_LAT), lat4(R_Q)
                for seg in range(2):
                    for h in range(HG):
                        a, b = seg * P, (seg + 1) * P
                        pe.matmul(ps[:, 4 + seg, h * P:(h + 1) * P], kf[:, h, a:b], q4[:, h, a:b], start=True, stop=False)
                        m = pe.matmul(ps[:, 4 + seg, h * P:(h + 1) * P], kb[:, h, a:b], q4[:, h, a:b],
                                      start=False, stop=True)
                m.then_inc(dg_mm, 1)
                xf, xb = lat4(R_T), lat4(R_T + E4)
                pe.wait_ge(x_mul, hg + 1)
                for h in range(HG):
                    pe.matmul(ps[:, 6, h * P:(h + 1) * P], xf[:, h, 0:P], xf[:, h, P:2 * P], start=True, stop=True)
                for h in range(HG):
                    m = pe.matmul(ps[:, 7, h * P:(h + 1) * P], xb[:, h, P:2 * P], xb[:, h, 0:P], start=True, stop=True)
                m.then_inc(x_mm, 1)
                for n in range(len(LEVELS)):
                    for d in range(2):
                        pe.wait_ge(l_mul, 2 * (hg * len(LEVELS) + n) + d + 1)
                        bank = 4 * (n % 2) + 2 * d
                        if n == 0 and d == 0:
                            pe.wait_ge(st_cp, 2 * hg + 2)
                        if n == 1:
                            pe.wait_ge(dg_out, hg + 1)
                            pe.wait_ge(x_cp, hg + 1)
                        if n >= 2:
                            pe.wait_ge(l_cp, 2 * (hg * len(LEVELS) + n - 2) + d + 1)
                        xx = (xf, xb)[d]
                        for seg in range(2):
                            for h in range(HG):
                                a, b = seg * P, (seg + 1) * P
                                m = pe.matmul(ps[:, bank + seg, h * P:(h + 1) * P], xx[:, h, a:b], xx[:, h, a:b],
                                              start=True, stop=True)
                        m.then_inc(l_mm, 1)
                pe.wait_ge(l_cp, 2 * (hg + 1) * len(LEVELS))
                pe.wait_ge(i_mul, hg + 1)
                s0, s1 = heads(R_KF, N_LAT, NT), heads(R_KB, N_LAT, NT)
                sf, sb_ = heads(R_LF, N_LAT, N_LAT + P), heads(R_LB, N_LAT, N_LAT + P)
                for h in range(HG):
                    dst = ps[:, h // 2, h % 2 * 256:h % 2 * 256 + 256]
                    pe.matmul(dst, ar(R_V + h * P, P), s0[:, h, :], start=True, stop=False)
                    pe.matmul(dst, ar(R_V + BANK + h * P, P), s1[:, h, :], start=False, stop=False)
                    pe.matmul(dst, sf[:, h, :], xf[:, h, :], start=False, stop=False)
                    m = pe.matmul(dst, sb_[:, h, :], xb[:, h, :], start=False, stop=True)
                m.then_inc(o_mm, 1)
                pe.wait_ge(o_sq, hg + 1)
                for hp in range(2):
                    m = pe.matmul(ps[:, 2 + hp, :], ones, ar(R_T + E4 + hp * BANK, BANK), start=True, stop=True)
                m.then_inc(o_sum, 1)

            u = U_OUT_ODD
            for blk in range(2):
                for k in range(4):
                    hi, lo = unit(u)
                    for kk in range(2):
                        kt = 2 * k + kk
                        if blk == 0:
                            pe.wait_ge(rlo_done, HEADS)
                        for n in range(4):
                            a, b = kk * BANK + n * P, kk * BANK + (n + 1) * P
                            dst = ps[:, 4 + 2 * blk + n // 2, n % 2 * 256:n % 2 * 256 + 256]
                            m = three(dst, hi[:, a:b], lo[:, a:b], s_hi[:, kt * N_LAT:(kt + 1) * N_LAT],
                                      s_lo[:, kt * N_LAT:(kt + 1) * N_LAT], kt == 0 and n % 2 == 0,
                                      kt == KT - 1 and n % 2 == 1, skip_group_check=True)
                    m.then_inc(pe_used, 1)
                    u += 1
            norm_sum(3, N_LAT)

            pe.wait_ge(rt_rdy, 1)
            pe.wait_ge(h_done, 4 * KT)
            for t in range(LT):
                for kt in range(KT):
                    m = three(ps[:, 0, t * N_EXP:(t + 1) * N_EXP], hh(kt, t * P, (t + 1) * P), hl(kt, t * P, (t + 1) * P),
                              rt_hi[:, kt * N_EXP:(kt + 1) * N_EXP], rt_lo[:, kt * N_EXP:(kt + 1) * N_EXP],
                              kt == 0, kt == KT - 1)
            m.then_inc(lg_mm, 1)
            n = 0
            for part in (h_hi, h_lo):
                for t in range(LT):
                    for kq in range(2):
                        if n >= 4:
                            pe.wait_ge(tk_out, n - 3)
                        for k in range(4):
                            kt = 4 * kq + k
                            m = pe.transpose(ps[:, 4 + n % 4, k * P:(k + 1) * P],
                                             part[:, kt * NT + t * P:kt * NT + (t + 1) * P].bitcast(F32), ident)
                        m.then_inc(tk_mm, 1)
                        n += 1
            pe.wait_ge(pick, 1)
            pe.matmul(ps[:, 1, 0:8], tri, route[:, 0, 32:40], start=True, stop=True)
            pe.matmul(ps[:, 1, 8:16], tri, route[:, 1, 32:40], start=True, stop=False)
            pe.matmul(ps[:, 1, 8:16], ones, route[:, 0, 32:40], start=False, stop=True)
            pe.matmul(ps[:, 1, 16:24], ones, route[:, 0, 32:40], start=True, stop=False)
            pe.matmul(ps[:, 1, 16:24], ones, route[:, 1, 32:40], start=False, stop=True).then_inc(rk_mm, 1)

            def gather():
                for q, part in enumerate((s_hi, s_lo)):
                    for kt in range(KT):
                        for t in range(LT):
                            m = pe.matmul(ps[:, 2 * q + kt // 4, kt % 4 * P:(kt % 4 + 1) * P],
                                          part[:, t * D + kt * P:t * D + (kt + 1) * P], onehot[:, t, :],
                                          start=(t == 0), stop=(t == LT - 1))
                return m

            def turn_hidden(i, cb):
                pe.wait_ge(eu_hid, i * CB + (cb + 1))
                if cb == 0:
                    pe.wait_ge(acc_rdy, i + 1)
                else:
                    pe.wait_ge(et_lo, i * CB + cb)
                for q in range(4):
                    m = pe.transpose(ps[:, 6, q * P:(q + 1) * P], ar(X_HID + q * P, P), ident)
                m.then_inc(et_mm, 1)

            pe.wait_ge(oh_rdy, 1)
            pe.wait_ge(tk_out, 8)
            gather().then_inc(ga_mm, 1)
            n_turns = pe.value_load(trips[0:1, 0:1], min_val=N_EXP, max_val=TURNS)
            with pe.Fori(0, n_turns) as i:
                past = i * EXP_UNITS
                pe.wait_ge(ga_lo, i + 1)
                v = 0
                for cb in range(CB):
                    bank = 2 * (cb % 2)
                    if cb == 1:
                        pe.wait_ge(acc_rdy, i + 1)
                    if cb >= 2:
                        pe.wait_ge(eu_hid, i * CB + (cb - 1))
                    for w in range(2):
                        for k in range(4):
                            hi, lo = unit(U_MOE + v, past)
                            for kk in range(2):
                                kt = 2 * k + kk
                                g = slice(2048 + kt * P, 2048 + (kt + 1) * P)
                                m = three(ps[:, bank + w, :], s_hi[:, g], s_lo[:, g], hi[:, kk * BANK:(kk + 1) * BANK],
                                          lo[:, kk * BANK:(kk + 1) * BANK], kt == 0, kt == KT - 1)
                            m.then_inc(pe_used, 1)
                            v += 1
                        if w == 0 and cb >= 1:
                            turn_hidden(i, cb - 1)
                    if cb == 1:
                        for t in range(LT):
                            pe.transpose(ps[:, 7, t * P:(t + 1) * P], onehot[:, t, :].bitcast(F32), ident)
                        for t in range(LT):
                            m = pe.matmul(ps[:, 7, 256:257], onehot[:, t, :].bitcast(F32), cw[:, t:t + 1],
                                          start=(t == 0), stop=(t == LT - 1))
                        m.then_inc(sp_mm, 1)
                for kt in range(EXP_KT):
                    if kt % 4 == 0:
                        pe.wait_ge(et_lo, i * CB + (kt // 4 + 1))
                    hi, lo = unit(U_MOE + v, past)
                    for n in range(2):
                        m = three(ps[:, 4 + n, :], h_hi[:, kt * P:(kt + 1) * P], h_lo[:, kt * P:(kt + 1) * P],
                                  hi[:, n * BANK:(n + 1) * BANK], lo[:, n * BANK:(n + 1) * BANK],
                                  kt == 0, kt == EXP_KT - 1)
                    m.then_inc(pe_used, 1)
                    v += 1
                    if kt == 3:
                        turn_hidden(i, CB - 1)
                    if kt == 11:
                        pe.wait_ge(oh_rdy, i + 2)
                        gather().then_inc(ga_mm, 1)
                pe.wait_ge(ey_lo, i * 2 + 2)
                pe.wait_ge(sp_rdy, i + 1)
                pe.wait_ge(ga_lo, i + 2)
                for n in range(KT):
                    dst = ps[:, (6, 7, 2, 3)[n // 2], n % 2 * 256:n % 2 * 256 + 256]
                    yh, yl = y_parts(n // 4)
                    pe.matmul(dst, yh[:, n % 4 * P:(n % 4 + 1) * P], spread[:, :], start=True, stop=False)
                    m = pe.matmul(dst, yl[:, n % 4 * P:(n % 4 + 1) * P], spread[:, :], start=False, stop=True)
                m.then_inc(sc_mm, 1)

            norm_sum(4, N_LAT)
            for n in range(4):
                for kt in (range(4), range(4, 8))[n % 2]:
                    pe.wait_ge(fin32, kt + 1)
                    t = n // 2
                    m = pe.transpose(ps[:, 4 + n, kt % 4 * P:(kt % 4 + 1) * P], xT[:, kt, t * P:(t + 1) * P], ident)
                m.then_inc(fin_tr, 1)

        @block.gpsimd
        def _(pool):
            pool.wait_ge(mask_in, 16)
            pool.tensor_copy(masks[:, :], ar(MASK_F, C_MASK)).then_inc(mask_rdy, 1)

        @block.scalar
        def _(act):
            split = [0]

            def hi(u, turn=0, per=0):
                act.wait_ge(raw_in[slot(u)], turn * (per // R * 16) + 16 * fills(u))
                if per or u >= R:
                    act.wait_ge(pe_used, turn * per + (u - R + 1))
                act.activation(w_hi[:, slot(u), :], raw[:, slot(u), :], ACT.Copy).then_inc(hi_done, 1)

            def split_to(n):
                while split[0] < n:
                    hi(split[0])
                    split[0] += 1

            def ada_rows(n, bank):
                act.wait_ge(pe_used, 4 * (n + 1) if n < 4 else U_ADA_C + 4 * (n - 3))
                if n >= 2:
                    act.wait_ge(ada_sel, n - 1)
                act.activation(ar(ADA_ROW + n % 2 * BANK, BANK)[0:4, :], ps[0:4, bank + n % 2, :],
                               ACT.Copy).then_inc(ada_row, 1)

            def squares(n, width):
                for kt in range(KT):
                    if n > 0 or kt >= 2:
                        act.wait_ge(sq_mm, KT * n + kt - 1)
                    act.activation(ar(NORM_AT[n] + kt % 2 * NT, width), xT[:, kt, 0:width],
                                   ACT.Square).then_inc(sq_done, 1)

            def norm_std(n, width):
                act.wait_ge(var_done, n + 1)
                act.activation(ar(NORM_AT[n] + 2 * NT, width), ar(NORM_AT[n] + 2 * NT, width),
                               ACT.Sqrt).then_inc(std_done, 1)

            def norm_hi(n, width):
                for kt in range(KT):
                    act.wait_ge(h32_done, KT * n + kt + 1)
                    act.activation(hh(kt, 0, width), ar(NORM_AT[n] + (3 + kt % 4) * NT, width),
                                   ACT.Copy).then_inc(hhi_done, 1)

            act.wait_ge(vec_out, 2)
            act.activation(sil[:, :], vT[:, V_C:V_C + 16], ACT.Silu).then_inc(silu_c, 1)
            act.wait_ge(silu_c, 1)
            cv = cond[:, 0:KT * 4].rearrange("p (k s) -> p s k", s=4)
            for s in range(2):
                act.activation(cv[:, s, :], sil[:, s * KT:(s + 1) * KT], ACT.Copy).then_inc(cond_hi, 1)
            act.wait_ge(lb_dif, 1)
            act.activation(lb[:, :], lb[:, :], ACT.Exp).then_inc(lb_exp, 1)
            for kt in range(KT):
                act.wait_ge(x_tr, kt + 1)
                act.activation(xT[:, kt, :], ps[:, (1 + kt) % 8, :], ACT.Copy).then_inc(x_out, 1)
            act.wait_ge(x_out, 8)

            for n in range(4):
                split_to(4 * n + 4 + LEAD)
                ada_rows(n, 0)
            squares(0, NT)
            norm_std(0, NT)
            norm_hi(0, NT)
            split_to(U_IN_EVEN + 8 + LEAD)
            act.wait_ge(pe_used, U_IN_EVEN + 8)
            for n in range(4):
                act.activation(ar(M_U + n * NT, NT), ps[:, 4 + n, :], ACT.Gelu).then_inc(u_out, 1)
            split_to(U_IN_EVEN + 12 + LEAD)
            act.wait_ge(pe_used, U_IN_EVEN + 12)
            act.wait_ge(mask_rdy, 1)
            for n in range(4):
                act.activation(ar(M_V + n * BANK, BANK), ps[:, n, :], ACT.Gelu).then_inc(v_out, 1)
            for n in range(4, 6):
                split_to(U_ADA_C + 4 * (n - 3) + LEAD)
                ada_rows(n, 4)
            act.wait_ge(lnv, 1)
            act.activation(rs[:, :], rs[:, :], ACT.Sqrt).then_inc(lns, 1)
            for n in range(8):
                act.wait_ge(dft_mm, n + 1)
                g, tp = n // 2, n % 2
                acs = ar(M_ACS, TT * A_G * 256).rearrange("p (t g c) -> p t g c", t=TT, g=A_G)
                act.activation(acs[:, 2 * tp:2 * tp + 2, g, :], ps[:, n, :].rearrange("p (t c) -> p t c", t=2),
                               ACT.Copy).then_inc(dft_out, 1)
            for g in range(4):
                act.wait_ge(y_mm, g + 1)
                act.activation(hh(g), ps[:, g, :], ACT.Copy).then_inc(yhi_done, 1)
            for h in range(4):
                act.wait_ge(y32_done, h + 1)
                act.activation(hh(4 + h), ar(M_TMP + h % 2 * NT, NT), ACT.Copy).then_inc(yhi_done, 1)
            split_to(U_OUT_EVEN + 8 + LEAD)
            act.wait_ge(resid, 8)
            with act.Fori(0, 2) as j:
                for n in range(3):
                    for k in range(4):
                        hi(U_ADA_E + LEAD + 4 * n + k, j, 12)
                    act.wait_ge(pe_used, j * 12 + (U_ADA_E + 4 * (n + 1)))
                    act.wait_ge(ada_sel, j * 3 + (6 + n))
                    act.activation(ar(ADA_ROW + n % 2 * BANK, BANK)[0:4, :], ps[0:4, n % 2, :],
                                   ACT.Copy).then_inc(ada_row, 1)
            split[0] = U_FFN + LEAD
            squares(1, NT)
            norm_std(1, NT)
            norm_hi(1, NT)
            u = U_FFN
            for first, count in FF_HALF:
                for it in range(first, first + count):
                    u += 4
                    split_to(u + LEAD)
                    act.wait_ge(pe_used, u)
                    if it >= 2:
                        act.wait_ge(hid_done, it - 1)
                    act.activation(ar(F_SIL + it % 2 * 1024, 1024), ps[:, 4 * (it % 2):4 * (it % 2) + 2, :],
                                   ACT.Silu).then_inc(up_silu, 1)
                act.wait_ge(hid_done, first + count)
                for f in range(2 * count):
                    fg = 2 * first + f
                    if f >= 6:
                        act.wait_ge(pe_used, u + f - 6 + 1)
                    act.activation(s_hi[:, f % 6 * NT:(f % 6 + 1) * NT], ar(F_HID + f * NT, NT),
                                   ACT.Copy).then_inc(hidhi, 1)
                    split_to(u + f + LEAD)
                u += 2 * count
            split_to(U_ADA_G + LEAD)
            act.wait_ge(resid, 24)
            with act.Fori(0, 4) as j:
                for n in range(3):
                    for k in range(4):
                        hi(U_ADA_G + LEAD + 4 * n + k, j, 12)
                    act.wait_ge(pe_used, j * 12 + (U_ADA_G + 4 * (n + 1)))
                    act.wait_ge(ada_sel, j * 3 + (12 + n))
                    act.activation(ar(ADA_ROW + n % 2 * BANK, BANK)[0:4, :], ps[0:4, n % 2, :],
                                   ACT.Copy).then_inc(ada_row, 1)
            split[0] = U_IN_ODD + LEAD
            squares(2, NT)
            norm_std(2, NT)
            norm_hi(2, NT)

            for hg in range(2):
                u = U_IN_ODD + 20 * hg
                split_to(u + 4 + LEAD)
                for d in range(2):
                    if d == 1:
                        split_to(u + 8 + LEAD)
                    act.wait_ge(z_clip, 2 * hg + d + 1)
                    act.activation(ar((R_KF, R_KB)[d], HG * NT), ar((R_LF, R_LB)[d], HG * NT), ACT.Exp,
                                   scale=-1.0).then_inc(z_exp, 1)
                split_to(u + 12 + LEAD)
                act.wait_ge(pe_used, u + 12)
                act.activation(ar(R_V, 4 * BANK), ps[:, 0:4, :], ACT.Copy).then_inc(v_rdy, 1)
                split_to(u + 16 + LEAD)
                for d in range(2):
                    act.wait_ge(f_rdy, 2 * hg + d + 1)
                    act.activation(ar(R_T, HG * NT), ar(R_T, HG * NT), ACT.Ln)
                    act.activation(ar((R_LF, R_LB)[d], HG * NT), ar((R_LF, R_LB)[d], HG * NT), ACT.Ln,
                                   scale=float(2 ** LN_CUT)).then_inc(ln_rdy, 1)
                split_to(u + 20 + LEAD)
                act.wait_ge(pe_used, u + 16)
                act.activation(lat4(R_Q), ps[:, 4:6, :].rearrange("p b (h t) -> p (b h) t", h=2),
                               ACT.Silu).then_inc(q_rdy, 1)
                act.wait_ge(pe_used, u + 20)
                act.activation(lat4(R_G), ps[:, 6:8, :].rearrange("p b (h t) -> p (b h) t", h=2),
                               ACT.Silu).then_inc(g_rdy, 1)

                tc = ar(R_T, 4 * 2 * P * 2).rearrange("p (d h t) -> p d h t", d=2, h=HG)
                act.wait_ge(gates, 2 * hg + 2)
                for d in range(2):
                    lg = heads((R_LF, R_LB)[d], N_LAT, NT)
                    for h in range(HG):
                        for seg in range(2):
                            if d == 0:
                                bias = tot[:, d, h, 5:6] if seg == 0 else tot[:, d, h, 3:4]
                            else:
                                bias = 0.0 if seg == 0 else tot[:, d, h, 2:3]
                            m = act.activation(tc[:, d, h, seg * P:(seg + 1) * P], lg[:, h, seg * P:(seg + 1) * P],
                                               ACT.Exp, bias=bias, scale=-1.0 if d == 0 else 1.0)
                    m.then_inc(c_exp, 1)
                for d in range(2):
                    act.wait_ge(st_mm, 2 * hg + d + 1)
                    act.activation(heads((R_LF, R_LB)[d], N_LAT, N_LAT + P),
                                   ps[:, 2 + d, :].rearrange("p (h c) -> p h c", h=HG), ACT.Copy).then_inc(st_cp, 1)
                lf, lbk = heads(R_LF, 0, N_LAT), heads(R_LB, 0, N_LAT)
                xf, xb = lat4(R_T), lat4(R_T + E4)
                act.wait_ge(st_mm, 2 * hg + 2)
                for h in range(HG):
                    act.activation(xf[:, h, 0:P], lf[:, h, 0:P], ACT.Exp, bias=tot[:, 0, h, 0:1], scale=-1.0)
                    act.activation(xb[:, h, 0:P], lbk[:, h, 0:P], ACT.Exp, bias=tot[:, 1, h, 0:1], scale=-1.0)
                act.activation(xf[:, :, P:2 * P], lf[:, :, P:2 * P], ACT.Exp)
                act.activation(xb[:, :, P:2 * P], lbk[:, :, P:2 * P], ACT.Exp).then_inc(x_exp, 1)
                for n in range(len(LEVELS)):
                    for d in range(2):
                        k = 2 * (hg * len(LEVELS) + n) + d
                        act.wait_ge(l_sub, k + 1)
                        act.activation(ar(R_T + d * E4, E4), ar(R_T + d * E4, E4), ACT.Exp).then_inc(l_exp, 1)
                act.wait_ge(l_mm, 2 * (hg + 1) * len(LEVELS))
                for h in range(HG):
                    act.activation(xf[:, h, P:2 * P], lf[:, h, P:2 * P], ACT.Exp, bias=tot[:, 0, h, 0:1])
                    act.activation(xb[:, h, 0:P], lbk[:, h, 0:P], ACT.Exp, bias=tot[:, 1, h, 4:5], scale=-1.0)
                    act.activation(xb[:, h, P:2 * P], lbk[:, h, P:2 * P], ACT.Exp, bias=tot[:, 1, h, 1:2], scale=-1.0)
                act.activation(xf[:, :, 0:P], lf[:, :, 0:P], ACT.Exp).then_inc(i_exp, 1)
                act.wait_ge(o_cp, hg + 1)
                act.activation(ar(R_T + E4, E4), ar(R_T, E4), ACT.Square).then_inc(o_sq, 1)
                act.wait_ge(o_var, hg + 1)
                act.activation(ar(R_T + E4, E4), ar(R_T + E4, E4), ACT.Sqrt).then_inc(o_std, 1)
                for h in range(HG):
                    act.wait_ge(r32_done, hg * HG + h + 1)
                    act.activation(s_hi[:, (hg * HG + h) * 256:(hg * HG + h + 1) * 256], lat4(R_T)[:, h, :],
                                   ACT.Copy).then_inc(rhi_done, 1)
            split_to(U_OUT_ODD + 8 + LEAD)

            act.wait_ge(resid, 32)
            squares(3, N_LAT)
            norm_std(3, N_LAT)
            norm_hi(3, N_LAT)
            act.wait_ge(rt_in, 16)
            act.activation(rt_hi[:, :], rt32[:, :], ACT.Copy).then_inc(rt_hid, 1)
            act.wait_ge(rt_dif, 1)
            act.activation(route[:, :, 50:51], route[:, :, 50:51], ACT.Exp).then_inc(rt_exp, 1)
            n = 0
            for part in (s_hi, s_lo):
                for t in range(LT):
                    for kq in range(2):
                        act.wait_ge(tk_mm, n + 1)
                        act.activation(part[:, t * D + kq * BANK:t * D + (kq + 1) * BANK], ps[:, 4 + n % 4, :],
                                       ACT.Copy).then_inc(tk_out, 1)
                        n += 1
            act.wait_ge(routed, 1)
            n_turns = act.value_load(trips[0:1, 0:1], min_val=N_EXP, max_val=TURNS)

            def gather_hi(k):
                act.wait_ge(ga_mm, k)
                act.activation(s_hi[:, 2048:3072], ps[:, 0:2, :], ACT.Copy).then_inc(ga_hi, 1)

            gather_hi(1)
            with act.Fori(0, n_turns) as i:
                def turned_hi(cb):
                    act.wait_ge(et_mm, i * CB + (cb + 1))
                    act.activation(h_hi[:, cb * BANK:(cb + 1) * BANK], ps[:, 6, :], ACT.Copy).then_inc(et_hi, 1)

                for v in range(EXP_UNITS):
                    hi(U_MOE + LEAD + v, i, EXP_UNITS)
                    if v < UP_UNITS and v % 8 == 3 and v > 8:
                        turned_hi(v // 8 - 1)
                    if v < UP_UNITS and v % 8 == 7:
                        act.wait_ge(pe_used, i * EXP_UNITS + (U_MOE + v + 1))
                        act.activation(ar(X_SIL, BANK), ps[:, 2 * (v // 8 % 2), :], ACT.Silu).then_inc(eu_silu, 1)
                    if v == UP_UNITS + 3:
                        turned_hi(CB - 1)
                    if v == UP_UNITS + 11:
                        gather_hi(i + 2)
                act.wait_ge(ey32, i + 1)
                for half in range(2):
                    act.activation(y_parts(half)[0], ar(X_Y + half * BANK, BANK), ACT.Copy).then_inc(ey_hi, 1)

            for kt in range(KT):
                act.wait_ge(resid, 32 + kt + 1)
                act.wait_ge(sq_mm, KT * 4 + kt - 1)
                act.activation(ar(NORM_AT[4] + kt % 2 * NT, N_LAT), xT[:, kt, 0:N_LAT], ACT.Square).then_inc(sq_done, 1)
            norm_std(4, N_LAT)
            for n in range(4):
                act.wait_ge(fin_tr, n + 1)
                m = act.activation(ar(X_OUT + n * BANK, BANK), ps[:, 4 + n, :], ACT.Copy)
                if n % 2:
                    m.then_inc(fin_out, 1)

        @block.vector
        def _(dve):
            split = [0]
            seq = [0]

            def link(ins):
                seq[0] += 1
                ins.then_inc(dve_seq, 1)
                dve.wait_ge(dve_seq, seq[0])

            def lo(u, plus=0):
                dve.wait_ge(hi_done, plus + (u + 1))
                dve.tensor_tensor(w_lo[:, slot(u), :], raw[:, slot(u), :], w_hi[:, slot(u), :].bitcast(F32),
                                  ALU.subtract).then_inc(lo_done, 1)

            def split_to(n):
                while split[0] < n:
                    lo(split[0])
                    split[0] += 1

            def ada_cols(n, bank, layer, at, number):
                dve.wait_ge(ada_sel, number)
                src = ps[:, sel_bank(n, bank), 0:8].rearrange("p (q s) -> p q s", s=2)
                dve.tensor_tensor(adaT[:, layer, at, :], src, bias[:, layer, at, :], ALU.add).then_inc(ada_done, 1)

            def norm_dve(n, width, layer, gain, sh, sc, streams):
                dve.wait_ge(sq_mm, KT * (n + 1))
                base = NORM_AT[n]
                inv = ar(base + 2 * NT, width)
                dve.tensor_scalar(inv, ps[:, 3, 0:width], 1.0 / D, EPS, ALU.mult, ALU.add).then_inc(var_done, 1)
                for s in range(2):
                    m = dve.scalar_tensor_tensor(coef[:, :, s], adaT[:, layer, sc * KT:(sc + 1) * KT, s], 1.0,
                                                 vT[:, gain + layer * KT:gain + (layer + 1) * KT], ALU.add, ALU.mult)
                link(m)
                dve.wait_ge(std_done, n + 1)
                link(dve.reciprocal(inv, inv))

                def lo_h(kt):
                    dve.wait_ge(hhi_done, KT * n + kt + 1)
                    dve.tensor_tensor(hl(kt, 0, width), ar(base + (3 + kt % 4) * NT, width),
                                      hh(kt, 0, width).bitcast(F32), ALU.subtract).then_inc(h_done, 1)

                for kt in range(KT):
                    if kt >= 2:
                        lo_h(kt - 2)
                    if kt >= 4:
                        dve.wait_ge(h_done, KT * n + kt - 3)
                    t = ar(base + (3 + kt % 4) * NT, width)
                    link(dve.tensor_tensor(t, xT[:, kt, 0:width], inv, ALU.mult))
                    for s in range(streams):
                        a, b = s * N_LAT, (s + 1) * N_LAT
                        m = dve.tensor_scalar(t[:, a:b], t[:, a:b], coef[:, kt, s:s + 1],
                                              adaT[:, layer, sh * KT + kt, s:s + 1], ALU.mult, ALU.add)
                    m.then_inc(h32_done, 1)
                lo_h(KT - 2)
                lo_h(KT - 1)

            def add_resid(kt, src, layer, gate, streams):
                for s in range(streams):
                    a, b = s * N_LAT, (s + 1) * N_LAT
                    m = dve.scalar_tensor_tensor(xT[:, kt, a:b], src[:, a:b],
                                                 adaT[:, layer, gate * KT + kt, s:s + 1], xT[:, kt, a:b],
                                                 ALU.mult, ALU.add)
                m.then_inc(resid, 1)

            dve.wait_ge(con_in, 16)
            dve.memset(cond[:, KT * 4:].bitcast(F32), 0.0).then_inc(vec_out, 1)
            dve.wait_ge(vec_tr, 1)
            dve.tensor_copy(vT[:, :], ps[:, 0, 0:V_ROWS])
            dve.tensor_copy(bT[:, :], ps[:, 0, 128:224]).then_inc(vec_out, 1)
            dve.wait_ge(vec_out, 2)
            bias = bT[:, :].rearrange("p (l v) -> p l v", l=2).unsqueeze(3).broadcast_to([P, 2, 48, 2])
            cv = cond[:, 0:KT * 4].rearrange("p (k s) -> p s k", s=4)
            for s in range(2):
                dve.wait_ge(cond_hi, 2)
                m = dve.tensor_tensor(cv[:, 2 + s, :], sil[:, s * KT:(s + 1) * KT], cv[:, s, :].bitcast(F32),
                                      ALU.subtract)
            m.then_inc(cond_rdy, 1)
            lbv = vT[:, V_LB:V_LB + 16]
            dve.tensor_tensor(lb[:, :], lbv, lbv, ALU.subtract).then_inc(lb_dif, 1)
            dve.wait_ge(lb_exp, 1)
            link(dve.reciprocal(lb1[:, :], lb[:, :]))
            link(dve.tensor_tensor(lb[:, :], lb[:, :], lb1[:, :], ALU.mult))
            link(dve.tensor_tensor(lb[:, :], lb[:, :], lb[:, :], ALU.subtract))
            link(dve.tensor_scalar(lb[:, :], lb[:, :], 0.0, 1.0, ALU.max, ALU.min))
            link(dve.tensor_scalar(lb1[:, :], lb[:, :], -1.0, 1.0, ALU.mult, ALU.add))

            for n in range(4):
                split_to(4 * n + 4 + LEAD)
                ada_cols(n, 0, 0, slice(4 * n, 4 * n + 4), n + 1)
            dve.wait_ge(ada_done, 4)
            norm_dve(0, NT, 0, V_NMIX, SH_M, SC_M, 2)

            split_to(U_IN_EVEN + 4 + LEAD)
            dve.wait_ge(pe_used, U_IN_EVEN + 4)
            for n in range(4):
                dve.tensor_copy(ar(M_A + n * NT, NT), ps[:, n, :]).then_inc(a_out, 1)
            split_to(U_IN_EVEN + 12 + LEAD)
            for t in range(TT):
                dve.wait_ge(v_out, t + 1)
                for h in range(B_H):
                    m = dve.bn_stats(stats[:, t * B_H + h, :], ar(M_V + t * BANK + h * P, P))
            link(m)
            for k in range(16):
                m = dve.bn_aggr(mv[:, k, :], stats[:, k, :])
            link(m)
            dve.tensor_scalar(rs[:, :], mv[:, :, 1], EPS, None, ALU.add).then_inc(lnv, 1)
            for n in range(4, 6):
                split_to(U_ADA_C + 4 * (n - 3) + LEAD)
                ada_cols(n, 4, 0, slice(4 * n, 4 * n + 4), n + 1)
            dve.wait_ge(lns, 1)
            link(dve.reciprocal(rs[:, :], rs[:, :]))
            for k in range(16):
                vt = ar(M_V + k * P, P)
                dve.tensor_scalar(vt, vt, mv[:, k, 0:1], rs[:, k:k + 1], ALU.subtract, ALU.mult).then_inc(ln_done, 1)
            for g in range(4):
                dve.wait_ge(yhi_done, g + 1)
                dve.tensor_tensor(hl(g), ps[:, g, :], hh(g).bitcast(F32), ALU.subtract).then_inc(ylo_done, 1)
            for h in range(4):
                dve.wait_ge(y_mm, 4 + h + 1)
                if h >= 2:
                    dve.wait_ge(ylo_done, 4 + h - 1)
                dve.tensor_tensor(ar(M_TMP + h % 2 * NT, NT), ps[:, 4 + h, :], ar(M_U + h * NT, NT),
                                  ALU.mult).then_inc(y32_done, 1)
                dve.wait_ge(yhi_done, 4 + h + 1)
                dve.tensor_tensor(hl(4 + h), ar(M_TMP + h % 2 * NT, NT), hh(4 + h).bitcast(F32),
                                  ALU.subtract).then_inc(ylo_done, 1)
            for blk in range(2):
                split_to(U_OUT_EVEN + 4 * blk + 4 + LEAD)
                dve.wait_ge(pe_used, U_OUT_EVEN + 4 * (blk + 1))
                for n in range(4):
                    add_resid(4 * blk + n, ps[:, 4 * blk + n, :], 0, G_M, 2)
            with dve.Fori(0, 2) as j:
                for n in range(3):
                    for k in range(4):
                        lo(U_ADA_E + LEAD + 4 * n + k, plus=j * 12)
                    ada_cols(n, 0, 0, bass.ds(j * 12 + (24 + 4 * n), 4), j * 3 + (7 + n))
            split[0] = U_FFN + LEAD
            dve.wait_ge(ada_done, 12)
            norm_dve(1, NT, 0, V_NFFN, SH_F, SC_F, 2)
            u = U_FFN
            for half, (first, count) in enumerate(FF_HALF):
                for it in range(first, first + count):
                    u += 4
                    split_to(u + LEAD)
                    dve.wait_ge(up_silu, it + 1)
                    f = it - first
                    dve.tensor_tensor(ar(F_HID + f * 1024, 1024).rearrange("p (b t) -> p b t", b=2),
                                      ps[:, 4 * (it % 2) + 2:4 * (it % 2) + 4, :],
                                      ar(F_SIL + it % 2 * 1024, 1024).rearrange("p (b t) -> p b t", b=2),
                                      ALU.mult).then_inc(hid_done, 1)
                for f in range(2 * count):
                    dve.wait_ge(hidhi, 2 * first + f + 1)
                    sl = slice(f % 6 * NT, (f % 6 + 1) * NT)
                    dve.tensor_tensor(s_lo[:, sl], ar(F_HID + f * NT, NT), s_hi[:, sl].bitcast(F32),
                                      ALU.subtract).then_inc(hidlo, 1)
                    split_to(u + f + LEAD)
                u += 2 * count
                split_to(u + LEAD)
                dve.wait_ge(pe_used, u)
                for n in range(KT):
                    add_resid(n, ps[:, n, :], 0, G_F, 2)
            with dve.Fori(0, 4) as j:
                for n in range(3):
                    for k in range(4):
                        lo(U_ADA_G + LEAD + 4 * n + k, plus=j * 12)
                    ada_cols(n, 0, 1, bass.ds(j * 12 + 4 * n, 4), j * 3 + (13 + n))
            split[0] = U_IN_ODD + LEAD
            dve.wait_ge(ada_done, 24)
            norm_dve(2, NT, 1, V_NMIX, SH_M, SC_M, 2)

            for hg in range(2):
                u = U_IN_ODD + 20 * hg
                for d in range(2):
                    split_to(u + 4 * d + 4 + LEAD)
                    dve.wait_ge(pe_used, u + 4 * d + 4)
                    dve.tensor_scalar(ar((R_LF, R_LB)[d], HG * NT).rearrange("p (h t) -> p h t", h=HG),
                                      ps[:, 4 * d:4 * d + 4, :], Z_MIN, None, ALU.max).then_inc(z_clip, 1)
                for d in range(2):
                    split_to(u + 8 + 4 * d + 4 + LEAD)
                    dve.wait_ge(z_exp, 2 * hg + d + 1)
                    kk, ll, tt = heads((R_KF, R_KB)[d]), heads((R_LF, R_LB)[d]), heads(R_T)
                    kfl, lfl, tfl = (ar(a, HG * NT) for a in ((R_KF, R_KB)[d], (R_LF, R_LB)[d], R_T))
                    link(dve.tensor_scalar(lfl, kfl, 1.0, None, ALU.add))
                    link(dve.reciprocal(lfl, lfl))
                    for h in range(HG):
                        col = d * HEADS + hg * HG + h
                        dve.scalar_tensor_tensor(kk[:, h, :], kk[:, h, :], lb1[:, col:col + 1], ll[:, h, :],
                                                 ALU.mult, ALU.mult)
                    for h in range(HG):
                        col = d * HEADS + hg * HG + h
                        m = dve.tensor_scalar(ll[:, h, :], ll[:, h, :], lb1[:, col:col + 1], lb[:, col:col + 1],
                                              ALU.mult, ALU.add)
                    link(m)
                    link(dve.tensor_scalar(tfl, lfl, float(2.0 ** -LN_CUT), None, ALU.max))
                    dve.tensor_scalar(lfl, lfl, F_FLOOR, float(2.0 ** -LN_CUT), ALU.max, ALU.min).then_inc(f_rdy, 1)
                    dve.wait_ge(ln_rdy, 2 * hg + d + 1)
                    link(dve.tensor_tensor(tfl, tfl, lfl, ALU.add))
                    if d == 1:
                        l4 = ar(R_LB, HG * NT).rearrange("p (s t) -> p s t", t=P)
                        link(dve.memset(l4[:, :, 0:1], 0.0))
                    for s in range(HG * TT):
                        a = s * P
                        if d == 0:
                            m = dve.tensor_tensor_scan(lfl[:, a:a + P], ones, tfl[:, a:a + P], 0.0, ALU.mult, ALU.add)
                        else:
                            m = dve.tensor_tensor_scan(lfl[:, a + 1:a + P], ones[:, 0:P - 1], tfl[:, a:a + P - 1], 0.0,
                                                       ALU.mult, ALU.add)
                    link(m)
                    l4 = lfl.rearrange("p (h s t) -> p h s t", h=HG, s=TT)
                    t4 = tfl.rearrange("p (h s t) -> p h s t", h=HG, s=TT)
                    if d == 0:
                        link(dve.tensor_copy(tot[:, d, :, 0:4], l4[:, :, :, P - 1]))
                    else:
                        link(dve.tensor_tensor(tot[:, d, :, 0:4], l4[:, :, :, P - 1], t4[:, :, :, P - 1], ALU.add))
                    for k in range(2):
                        m = dve.tensor_tensor(tot[:, d, :, 4 + k:5 + k], tot[:, d, :, 2 * k:2 * k + 1],
                                              tot[:, d, :, 2 * k + 1:2 * k + 2], ALU.add)
                    m.then_inc(gates, 1)
                split_to(u + 20 + LEAD)
                tc = ar(R_T, 2 * HG * 256).rearrange("p (d h t) -> p d h t", d=2, h=HG)
                for d in range(2):
                    dve.wait_ge(c_exp, 2 * hg + 2)
                    kb = heads((R_KF, R_KB)[d], N_LAT, NT)
                    dve.tensor_tensor(kb, kb, tc[:, d], ALU.mult).then_inc(c_mul, 1)
                for d in range(2):
                    dve.wait_ge(c_tr, 2 * hg + d + 1)
                    if d == 0:
                        dve.wait_ge(c_mul, 2 * hg + 2)
                    else:
                        dve.wait_ge(st_mm, 2 * hg + 1)
                    dve.tensor_copy(ar(R_T, 2 * BANK).rearrange("p (s c) -> p s c", s=2), ps[:, 0:2, :]).then_inc(c_cp, 1)
                dve.wait_ge(q_rdy, hg + 1)
                q4 = lat4(R_Q)
                s01 = (heads(R_KF, N_LAT, NT), heads(R_KB, N_LAT, NT))
                kf, kb = heads(R_KF, 0, N_LAT), heads(R_KB, 0, N_LAT)
                xf, xb = lat4(R_T), lat4(R_T + E4)
                dve.wait_ge(dg_mm, hg + 1)
                id4 = ident.unsqueeze(1).broadcast_to([P, HG, P])
                for seg in range(2):
                    m = dve.tensor_tensor(s01[seg][:, :, seg * P:(seg + 1) * P],
                                          ps[:, 4 + seg, :].rearrange("p (h t) -> p h t", h=HG), id4, ALU.mult)
                m.then_inc(dg_out, 1)
                dve.wait_ge(x_exp, hg + 1)
                dve.tensor_tensor(xf[:, :, 0:P], xf[:, :, 0:P], kf[:, :, 0:P], ALU.mult)
                dve.tensor_tensor(xf[:, :, P:2 * P], xf[:, :, P:2 * P], q4[:, :, P:2 * P], ALU.mult)
                dve.tensor_tensor(xb[:, :, 0:P], xb[:, :, 0:P], q4[:, :, 0:P], ALU.mult)
                dve.tensor_tensor(xb[:, :, P:2 * P], xb[:, :, P:2 * P], kb[:, :, P:2 * P], ALU.mult).then_inc(x_mul, 1)
                dve.wait_ge(x_mm, hg + 1)
                dve.tensor_copy(s01[0][:, :, P:2 * P], ps[:, 6, :].rearrange("p (h t) -> p h t", h=HG))
                dve.tensor_copy(s01[1][:, :, 0:P], ps[:, 7, :].rearrange("p (h t) -> p h t", h=HG)).then_inc(x_cp, 1)

                def level_parts(at, hs):
                    v = ar(at, HG * NT).rearrange("p (h t) -> p h t", h=HG)[:, :, 0:N_LAT]
                    return v.rearrange("p h (b c) -> p h b c", c=2 * hs)

                def temp_parts(at, hs):
                    return ar(at, E4).rearrange("p (h b c) -> p h b c", h=HG, c=2 * hs)

                def masked(n, d):
                    dve.wait_ge(l_mm, 2 * (hg * len(LEVELS) + n) + d + 1)
                    if hg == 0 and n + d == 0:
                        dve.wait_ge(mask_rdy, 1)
                    if n + d > 0:
                        dve.wait_ge(l_cp, 2 * (hg * len(LEVELS) + n) + d)
                    else:
                        dve.wait_ge(dg_out, hg + 1)
                        dve.wait_ge(x_cp, hg + 1)
                    mk = masks[:, (2 * n + d) * P:(2 * n + d + 1) * P].unsqueeze(1).broadcast_to([P, HG, P])
                    for seg in range(2):
                        m = dve.copy_predicated(s01[seg][:, :, seg * P:(seg + 1) * P], mk,
                                                ps[:, 4 * (n % 2) + 2 * d + seg, :].rearrange("p (h t) -> p h t", h=HG))
                    m.then_inc(l_cp, 1)

                for n, hs in enumerate(LEVELS):
                    nb = N_LAT // (2 * hs)
                    for d in range(2):
                        if n >= 1:
                            dve.wait_ge(l_mm, 2 * (hg * len(LEVELS) + n - 1) + d + 1)
                        ll, xx = level_parts((R_LF, R_LB)[d], hs), temp_parts(R_T + d * E4, hs)
                        r = hs - 1 if d == 0 else hs
                        ref = ll[:, :, :, r:r + 1].broadcast_to([P, HG, nb, hs])
                        dve.tensor_tensor(xx[:, :, :, 0:hs], ref, ll[:, :, :, 0:hs], ALU.subtract)
                        dve.tensor_tensor(xx[:, :, :, hs:], ll[:, :, :, hs:], ref, ALU.subtract).then_inc(l_sub, 1)
                    for d in range(2):
                        if n >= 1:
                            masked(n - 1, d)
                    for d in range(2):
                        dve.wait_ge(l_exp, 2 * (hg * len(LEVELS) + n) + d + 1)
                        xx = temp_parts(R_T + d * E4, hs)
                        kq = level_parts((R_KF, R_KB)[d], hs), temp_parts(R_Q, hs)
                        left, right = kq if d == 0 else kq[::-1]
                        dve.tensor_tensor(xx[:, :, :, 0:hs], xx[:, :, :, 0:hs], left[:, :, :, 0:hs], ALU.mult)
                        dve.tensor_tensor(xx[:, :, :, hs:], xx[:, :, :, hs:], right[:, :, :, hs:],
                                          ALU.mult).then_inc(l_mul, 1)
                for d in range(2):
                    masked(len(LEVELS) - 1, d)
                dve.wait_ge(i_exp, hg + 1)
                dve.tensor_tensor(ar(R_T, E4), ar(R_T, E4), ar(R_Q, E4), ALU.mult)
                dve.tensor_tensor(ar(R_T + E4, E4), ar(R_T + E4, E4), ar(R_Q, E4), ALU.mult).then_inc(i_mul, 1)
                dve.wait_ge(o_mm, hg + 1)
                dve.tensor_scalar(ar(R_T, E4).rearrange("p (b t) -> p b t", b=2), ps[:, 0:2, :], P ** -0.5, None,
                                  ALU.mult).then_inc(o_cp, 1)
                dve.wait_ge(o_sum, hg + 1)
                dve.tensor_scalar(ar(R_T + E4, E4).rearrange("p (b t) -> p b t", b=2), ps[:, 2:4, :], 1.0 / P, EPS,
                                  ALU.mult, ALU.add).then_inc(o_var, 1)
                dve.wait_ge(o_std, hg + 1)
                link(dve.reciprocal(ar(R_T + E4, E4), ar(R_T + E4, E4)))
                link(dve.tensor_tensor(ar(R_T, E4), ar(R_T, E4), ar(R_T + E4, E4), ALU.mult))
                for h in range(HG):
                    col = V_RNORM + hg * HG + h
                    dve.scalar_tensor_tensor(lat4(R_T)[:, h, :], lat4(R_T)[:, h, :], vT[:, col:col + 1],
                                             lat4(R_G)[:, h, :], ALU.mult, ALU.mult).then_inc(r32_done, 1)
                for h in range(HG):
                    k = hg * HG + h
                    dve.wait_ge(rhi_done, k + 1)
                    dve.tensor_tensor(s_lo[:, k * 256:(k + 1) * 256], lat4(R_T)[:, h, :],
                                      s_hi[:, k * 256:(k + 1) * 256].bitcast(F32), ALU.subtract).then_inc(rlo_done, 1)
            split_to(U_OUT_ODD + 8 + LEAD)
            for blk in range(2):
                dve.wait_ge(pe_used, U_OUT_ODD + 4 * (blk + 1))
                for n in range(4):
                    add_resid(4 * blk + n, ps[:, 4 + 2 * blk + n // 2, n % 2 * 256:n % 2 * 256 + 256], 1, G_M, 1)
            norm_dve(3, N_LAT, 1, V_NFFN, SH_F, SC_F, 1)

            dve.wait_ge(rt_hid, 1)
            dve.tensor_tensor(rt_lo[:, :], rt32[:, :], rt_hi[:, :].bitcast(F32), ALU.subtract).then_inc(rt_rdy, 1)
            dve.wait_ge(lg_mm, 1)
            link(dve.tensor_copy(route[:, :, 0:8], ps[:, 0, 0:16].rearrange("p (t e) -> p t e", e=8)))
            for t in range(LT):
                m = dve.max(route[:, t, 8:16], route[:, t, 0:8])
            link(m)
            for t in range(LT):
                m = dve.max_index(idx[:, t, :], route[:, t, 8:16], route[:, t, 0:8])
            link(m)
            link(dve.tensor_copy(route[:, :, 16:18], idx[:, :, 0:2]))
            dve.tensor_tensor(route[:, :, 50:51], route[:, :, 9:10], route[:, :, 8:9], ALU.subtract).then_inc(rt_dif, 1)
            for t in range(LT):
                for k in range(2):
                    at = (18, 40)[k]
                    m = dve.tensor_scalar(route[:, t, at:at + 8], iota[:, 0:8], route[:, t, 16 + k:17 + k], None,
                                          ALU.is_equal)
            link(m)
            dve.tensor_tensor(route[:, :, 32:40], route[:, :, 18:26], route[:, :, 40:48], ALU.add).then_inc(pick, 1)
            dve.wait_ge(pick, 1)
            dve.wait_ge(rt_exp, 1)
            link(dve.tensor_scalar(route[:, :, 51:52], route[:, :, 50:51], 1.0, None, ALU.add))
            link(dve.reciprocal(route[:, :, 51:52], route[:, :, 51:52]))
            link(dve.tensor_tensor(route[:, :, 52:53], route[:, :, 50:51], route[:, :, 51:52], ALU.mult))
            for t in range(LT):
                m = dve.tensor_scalar(route[:, t, 18:26], route[:, t, 18:26], route[:, t, 51:52], None, ALU.mult)
            link(m)
            for t in range(LT):
                m = dve.scalar_tensor_tensor(comb[:, t, 0:N_EXP], route[:, t, 40:48], route[:, t, 52:53],
                                             route[:, t, 18:26], ALU.mult, ALU.add)
            dve.wait_ge(rk_mm, 1)
            link(dve.tensor_scalar(route[:, :, 53:61], route[:, :, 32:40], -1024.0, 1024.0, ALU.mult, ALU.add))
            link(dve.tensor_tensor(rank[:, :, 0:8], ps[:, 1, 0:16].rearrange("p (t e) -> p t e", e=8),
                                   route[:, :, 53:61], ALU.add))
            dve.memset(rank[:, :, TURNS:], 1024.0)
            dve.memset(comb[:, :, TURNS:], 0.0)
            sel, order = over[:, O_SEL:O_SEL + N_EXP], over[:, O_ORDER:O_ORDER + N_EXP]
            link(dve.tensor_scalar(sel, ps[:, 1, 16:24], float(SLOTS), None, ALU.is_gt))
            link(dve.tensor_tensor_scan(order, ones[:, 0:N_EXP], sel, 0.0, ALU.mult, ALU.add))
            dve.tensor_copy(cnt[:, T_OVER:T_OVER + 1], order[:, N_EXP - 1:N_EXP])
            link(dve.tensor_scalar(cnt[:, T_TURNS:T_TURNS + 1], order[:, N_EXP - 1:N_EXP], float(N_EXP), None, ALU.add))
            pick_over = over[:, O_PICK:O_PICK + N_OVER * N_EXP].rearrange("p (j e) -> p j e", e=N_EXP)
            for j in range(N_OVER):
                m = dve.scalar_tensor_tensor(pick_over[:, j, :], order, float(j + 1), sel, ALU.is_equal, ALU.mult)
            link(m)
            tmp = over[:, O_TMP:].rearrange("p (t j e) -> p t j e", t=LT, e=N_EXP)
            link(dve.tensor_tensor(tmp[:, 0], pick_over, iota[:, 0:N_EXP].unsqueeze(1).broadcast_to([P, N_OVER, N_EXP]),
                                   ALU.mult))
            link(dve.tensor_reduce(cnt[:, T_EXPERT:].unsqueeze(2), tmp[:, 0], AX.X, ALU.add))
            for full in (rank, comb):
                for t in range(LT):
                    m = dve.tensor_tensor(tmp[:, t], pick_over,
                                          full[:, t, 0:N_EXP].unsqueeze(1).broadcast_to([P, N_OVER, N_EXP]), ALU.mult)
                link(m)
                for t in range(LT):
                    m = dve.tensor_reduce(full[:, t, N_EXP:TURNS].unsqueeze(2), tmp[:, t], AX.X, ALU.add)
                link(m)
            link(dve.tensor_scalar(rank[:, :, N_EXP:TURNS], rank[:, :, N_EXP:TURNS], -float(SLOTS), None, ALU.add))
            link(dve.tensor_copy(trips[:, :], cnt[:, :]))
            dve.memset(ar(X_ACC, KT * N_LAT), 0.0).then_inc(acc_rdy, 1)
            dve.memset(cslot[:, :], 0.0).then_inc(routed, 1)
            dve.wait_ge(routed, 1)

            def gather_lo(k):
                dve.wait_ge(ga_hi, k)
                dve.tensor_copy(s_lo[:, 2048:3072], ps[:, 2:4, :]).then_inc(ga_lo, 1)

            def one_hots(i):
                for t in range(LT):
                    dve.tensor_scalar(onehot[:, t, :], iota, rank[:, t, bass.ds(i, 1)] if not isinstance(i, int)
                                      else rank[:, t, i:i + 1], None, ALU.is_equal)
                src = comb[:, :, bass.ds(i, 1)] if not isinstance(i, int) else comb[:, :, i:i + 1]
                dve.tensor_copy(cw[:, :].unsqueeze(2), src).then_inc(oh_rdy, 1)

            one_hots(0)
            gather_lo(1)
            n_turns = dve.value_load(trips[0:1, 0:1], min_val=N_EXP, max_val=TURNS)
            acc = ar(X_ACC, KT * N_LAT)
            with dve.Fori(0, n_turns) as i:
                past = i * EXP_UNITS

                def turned_lo(cb):
                    dve.wait_ge(et_hi, i * CB + (cb + 1))
                    dve.tensor_tensor(h_lo[:, cb * BANK:(cb + 1) * BANK], ps[:, 6, :],
                                      h_hi[:, cb * BANK:(cb + 1) * BANK].bitcast(F32), ALU.subtract).then_inc(et_lo, 1)

                for v in range(EXP_UNITS):
                    lo(U_MOE + LEAD + v, plus=past)
                    if v < UP_UNITS and v % 8 == 3 and v > 8:
                        turned_lo(v // 8 - 1)
                    if v < UP_UNITS and v % 8 == 7:
                        dve.wait_ge(eu_silu, i * CB + (v // 8 + 1))
                        dve.tensor_tensor(ar(X_HID, BANK), ps[:, 2 * (v // 8 % 2) + 1, :], ar(X_SIL, BANK),
                                          ALU.mult).then_inc(eu_hid, 1)
                    if v == 17:
                        dve.wait_ge(sp_mm, i + 1)
                        dve.tensor_copy(spread[:, :], ps[:, 7, 0:256])
                        dve.tensor_copy(cslot[:, :], ps[:, 7, 256:257]).then_inc(sp_rdy, 1)
                    if v == UP_UNITS + 3:
                        turned_lo(CB - 1)
                    if v == UP_UNITS + 5:
                        one_hots(i + 1)
                    if v == UP_UNITS + 11:
                        gather_lo(i + 2)
                dve.wait_ge(pe_used, past + (U_MOE + EXP_UNITS))
                dve.wait_ge(sp_rdy, i + 1)
                dve.tensor_scalar(ar(X_Y, D).rearrange("p (b t) -> p b t", b=2), ps[:, 4:6, :], cslot[:, 0:1], None,
                                  ALU.mult).then_inc(ey32, 1)
                for half in range(2):
                    yh, yl = y_parts(half)
                    dve.wait_ge(ey_hi, i * 2 + (half + 1))
                    dve.tensor_tensor(yl, ar(X_Y + half * BANK, BANK), yh.bitcast(F32), ALU.subtract).then_inc(ey_lo, 1)
                dve.wait_ge(sc_mm, i + 1)
                dve.tensor_tensor(acc[:, 0:1024].rearrange("p (b t) -> p b t", b=2),
                                  acc[:, 0:1024].rearrange("p (b t) -> p b t", b=2), ps[:, 6:8, :], ALU.add)
                dve.tensor_tensor(acc[:, 1024:2048].rearrange("p (b t) -> p b t", b=2),
                                  acc[:, 1024:2048].rearrange("p (b t) -> p b t", b=2), ps[:, 2:4, :],
                                  ALU.add).then_inc(acc_rdy, 1)

            dve.wait_ge(acc_rdy, n_turns + 1)
            for n in range(KT):
                add_resid(n, acc[:, n * N_LAT:(n + 1) * N_LAT], 1, G_F, 1)
            dve.wait_ge(sq_mm, KT * 5)
            inv = ar(NORM_AT[4] + 2 * NT, N_LAT)
            dve.tensor_scalar(inv, ps[:, 3, 0:N_LAT], 1.0 / D, EPS, ALU.mult, ALU.add).then_inc(var_done, 1)
            dve.wait_ge(std_done, 5)
            link(dve.reciprocal(inv, inv))
            for kt in range(KT):
                dve.scalar_tensor_tensor(xT[:, kt, 0:N_LAT], xT[:, kt, 0:N_LAT], vT[:, V_NOUT + kt:V_NOUT + kt + 1], inv,
                                         ALU.mult, ALU.mult).then_inc(fin32, 1)


_INS = ["x", "c", "ctx", "c_ctx", "w_ada", "b_ada", "norm_mix", "norm_ffn", "norm_out", "w_in_even", "gmlp_w",
        "gmlp_b", "w_out_even", "w_in_odd", "rec_lb", "rec_norm", "w_out_odd", "ffn_w1", "ffn_w3", "ffn_w2",
        "router_w", "moe_w1", "moe_w3", "moe_w2"]


def kernel(**inputs):
    import concourse.bacc as _bacc
    from concourse.bass_utils import run_bass_kernel_spmd as _run

    nc = _bacc.Bacc("TRN2", target_bir_lowering=False, num_devices=1, dynamic_dma_scratch_size=1024)
    arrays, args = {}, []
    for name in _INS:
        a = np.asarray(inputs[name])
        if name == "gmlp_w":
            a = a[0].transpose(2, 0, 1)
        a = np.ascontiguousarray(a)
        arrays[f"in_{name}"] = a
        args.append(nc.dram_tensor(f"in_{name}", a.shape, mybir.dt.from_np(a.dtype), kind="ExternalInput").ap())
    for name, a in zip(("cst", "msk"), constants()):
        arrays[name] = a
        args.append(nc.dram_tensor(name, a.shape, mybir.dt.from_np(a.dtype), kind="ExternalInput").ap())
    args.append(nc.dram_tensor("out", (1, N_LAT, D), F32, kind="ExternalOutput").ap())
    build(nc, *args)
    return _run(nc, [arrays], core_ids=[0]).results[0]["out"]
```

```python
from contextlib import ExitStack

import numpy as np

import concourse.bass as bass
from concourse import mybir

F32 = mybir.dt.float32
F32R = mybir.dt.float32r
U8 = mybir.dt.uint8
U32 = mybir.dt.uint32
I32 = mybir.dt.int32
ALU = mybir.AluOpType
ACT = mybir.ActivationFunctionType
AX = mybir.AxisListType

P = 128
D = 1024
KT = D // P
N_LAT = 256
N_CTX = 256
NT = N_LAT + N_CTX
TT = NT // P
LT = N_LAT // P
A_G = 4
B_H = 4
HEADS = 8
HG = 2
NG = HEADS // HG
G_UNITS = 10
R_W = HEADS * P
D_FF = 2816
N_EXP = 8
D_EXP = 3584
EPS = 1e-6
F_FLOOR = 1e-30
LN_FLOOR = float(np.log(F_FLOOR))
LN_MAX = 43.0
BANK = 512

UNIT = 1024
R = 6
LEAD = 5

FF_COLS = 256
FF_IT = D_FF // FF_COLS
FF_HALF = [(0, 6), (6, FF_IT - 6)]
CB = D_EXP // BANK
EXP_KT = D_EXP // P
UP_UNITS = CB * 8
EXP_UNITS = UP_UNITS + EXP_KT

U_ADA_A = 0
U_IN_EVEN = U_ADA_A + 16
U_ADA_C = U_IN_EVEN + 12
U_OUT_EVEN = U_ADA_C + 8
U_ADA_E = U_OUT_EVEN + 8
U_FFN = U_ADA_E + 24
U_ADA_G = U_FFN + FF_IT * 6
U_IN_ODD = U_ADA_G + 48
U_OUT_ODD = U_IN_ODD + 40
U_MOE = U_OUT_ODD + 8

C_ID, C_ONE, C_IOTA, C_TRI, C_SEL = 0, 128, 256, 384, 512
C_RES = 514
DFT_CS, DFT_CT, DFT_ST = 0, 256, 768
C_DFT = 1280
LEVELS = [64, 32, 16, 8, 4, 2, 1]
C_MASK = len(LEVELS) * P

V_C, V_CC, V_NMIX, V_NFFN, V_NOUT, V_LB, V_RNORM, V_ROWS = 0, 8, 16, 32, 48, 56, 72, 80
SH_M, SC_M, G_M, SH_F, SC_F, G_F = range(6)

ARENA = 14336
X_ROWS = 0
M_A, M_U, M_V, M_ACS, M_GW, M_DFT, M_TMP = 0, 2048, 4096, 6144, 10240, 10752, 12032
MASK_F = 4096
VEC_ROWS, B_ROWS = 12544, 12672
ADA_ROW = 13312
RESID_AT = [0, 0, 16, 24, 32]
NORM_AT = [6144, 8192, 8192, 8192, 8192]
F_HID, F_SIL = 0, 6144
G_LAT = HG * N_LAT
R_KF, R_LF, R_KB, R_LB, R_V, R_T, R_Q, R_G = (G_LAT * k for k in (0, 2, 4, 6, 8, 10, 12, 13))
R_SET = 14 * G_LAT
X_ACC, X_HID, X_SIL, X_Y, X_OUT = 0, 2048, 2560, 3072, 4096
SLOTS = 128
N_OVER = 2 * N_LAT // (SLOTS + 1)
TURNS = N_EXP + N_OVER
T_TURNS, T_OVER, T_EXPERT = 0, 1, 2
O_SEL, O_ORDER, O_PICK, O_TMP = 0, 8, 16, 16 + 8 * N_OVER


def constants():
    i = np.arange(P)
    c = np.zeros((P, C_RES + C_DFT), np.float32)
    c[:, C_ID:C_ID + P] = np.eye(P)
    c[:, C_ONE:C_ONE + P] = 1.0
    c[:, C_IOTA:C_IOTA + P] = i[None, :]
    c[:, C_TRI:C_TRI + P] = i[:, None] < i[None, :]
    c[[0, 2], C_SEL] = 1.0
    c[[1, 3], C_SEL + 1] = 1.0
    d = c[:, C_RES:]
    w = 2 * np.pi / P * ((i[:, None] * i[None, :]) % P)
    scale = 1.0 / np.sqrt(N_LAT * P)
    d[:, DFT_CS:DFT_CS + P] = np.cos(w) * scale
    d[:, DFT_CS + P:DFT_CS + 2 * P] = np.sin(w) * scale
    t = np.arange(N_LAT)
    w = 2 * np.pi / N_LAT * ((t[:, None] * t[None, :]) % N_LAT)
    for tt in range(LT):
        d[:, DFT_CT + tt * N_LAT:DFT_CT + (tt + 1) * N_LAT] = np.cos(w[tt * P:(tt + 1) * P])
        d[:, DFT_ST + tt * N_LAT:DFT_ST + (tt + 1) * N_LAT] = -np.sin(w[tt * P:(tt + 1) * P])
    m = np.zeros((P, len(LEVELS), P), np.float32)
    for n, h in enumerate(LEVELS):
        block, side = i // (2 * h), i // h % 2
        m[:, n] = (block[:, None] == block[None, :]) & (side[:, None] != side[None, :])
    return c, m.reshape(P, -1)


def build(nc, x, c, ctx_in, c_ctx, w_ada, b_ada, norm_mix, norm_ffn, norm_out, w_in_even, gmlp_wt, gmlp_b,
          w_out_even, w_in_odd, rec_lb, rec_norm, w_out_odd, ffn_w1, ffn_w3, ffn_w2, router_w,
          moe_w1, moe_w3, moe_w2, cst, msk, out):
    es = ExitStack()
    with es:
        def sb(name, shape, dt=F32):
            return es.enter_context(nc.sbuf_tensor(name, shape, dt))

        def sem(name):
            return es.enter_context(nc.semaphore(name))

        raw = sb("raw", [P, R, UNIT])
        w_hi = sb("w_hi", [P, R, UNIT], F32R)
        w_lo = sb("w_lo", [P, R, UNIT], F32R)
        xT = sb("xT", [P, KT, NT])
        h_hi = sb("h_hi", [P, KT * NT], F32R)
        h_lo = sb("h_lo", [P, KT * NT], F32R)
        s_hi = sb("s_hi", [P, 3072], F32R)
        s_lo = sb("s_lo", [P, 3072], F32R)
        arena = sb("arena", [P, ARENA])
        con = sb("con", [P, C_RES])
        masks = sb("masks", [P, C_MASK], U8)
        vT = sb("vT", [P, V_ROWS])
        bT = sb("bT", [P, 96])
        sil = sb("sil", [P, 16])
        cond = sb("cond", [P, KT * 4 + P], F32R)
        adaT = sb("adaT", [P, 2, 48, 2])
        coef = sb("coef", [P, KT, 2])
        stats = sb("stats", [P, 16, 6])
        mv = sb("mv", [P, 16, 2])
        rs = sb("rs", [P, 16])
        lb = sb("lb", [P, 16])
        lb1 = sb("lb1", [P, 16])
        tot = sb("tot", [P, 2, 2, HG, 6])
        temp2 = sb("temp2", [P, 2 * G_LAT])
        temp3 = sb("temp3", [P, HG * NT])
        rt32 = sb("rt32", [P, KT * N_EXP])
        rt_hi = sb("rt_hi", [P, KT * N_EXP], F32R)
        rt_lo = sb("rt_lo", [P, KT * N_EXP], F32R)
        route = sb("route", [P, LT, 64])
        idx = sb("idx", [P, LT, 8], U32)
        rank = sb("rank", [P, LT, TURNS + 1])
        comb = sb("comb", [P, LT, TURNS + 1])
        trips = sb("trips", [P, T_EXPERT + N_OVER], I32)
        cnt = sb("cnt", [P, T_EXPERT + N_OVER])
        over = sb("over", [P, O_TMP + LT * N_OVER * N_EXP])
        onehot = sb("onehot", [P, LT, SLOTS], F32R)
        spread = sb("spread", [P, N_LAT], F32R)
        cw = sb("cw", [P, LT])
        cslot = sb("cslot", [P, 1])
        y_hi = sb("y_hi", [P, BANK], F32R)
        y_lo = sb("y_lo", [P, BANK], F32R)
        ps = es.enter_context(nc.psum_tensor("ps", [P, 8, BANK], F32))

        ident = con[:, C_ID:C_ID + P]
        ones = con[:, C_ONE:C_ONE + P]
        iota = con[:, C_IOTA:C_IOTA + P]
        tri = con[:, C_TRI:C_TRI + P]

        def ar(at, n):
            return arena[:, at:at + n]

        gb_row = arena[32:33, ADA_ROW:ADA_ROW + B_H * P]

        def hh(kt, a=0, b=NT):
            return h_hi[:, kt * NT + a:kt * NT + b]

        def hl(kt, a=0, b=NT):
            return h_lo[:, kt * NT + a:kt * NT + b]

        def y_parts(half):
            at = EXP_KT * P
            return ((h_hi[:, at:at + BANK], h_lo[:, at:at + BANK]), (y_hi[:, :], y_lo[:, :]))[half]

        raw_in = [sem(f"raw_in{k}") for k in range(R)]
        hi_done, lo_done, pe_used = sem("hi_done"), sem("lo_done"), sem("pe_used")
        vec_in, con_in, x_in, mix_in, rt_in = sem("vec_in"), sem("con_in"), sem("x_in"), sem("mix_in"), sem("rt_in")
        mask_in, mask_rdy = sem("mask_in"), sem("mask_rdy")
        vec_tr, vec_out, x_tr, x_out = sem("vec_tr"), sem("vec_out"), sem("x_tr"), sem("x_out")
        silu_c, cond_hi, cond_rdy, dve_seq = sem("silu_c"), sem("cond_hi"), sem("cond_rdy"), sem("dve_seq")
        lb_dif, lb_exp = sem("lb_dif"), sem("lb_exp")
        ada_row, ada_sel, ada_done = sem("ada_row"), sem("ada_sel"), sem("ada_done")
        sq_done, sq_mm, var_done, std_done = sem("sq_done"), sem("sq_mm"), sem("var_done"), sem("std_done")
        h32_done, hhi_done, h_done = sem("h32_done"), sem("hhi_done"), sem("h_done")
        a_out, u_out, v_out = sem("a_out"), sem("u_out"), sem("v_out")
        lnv, lns, ln_done = sem("lnv"), sem("lns"), sem("ln_done")
        dft_mm, dft_out, y_mm = sem("dft_mm"), sem("dft_out"), sem("y_mm")
        y32_done, yhi_done, ylo_done = sem("y32_done"), sem("yhi_done"), sem("ylo_done")
        resid = sem("resid")
        up_silu, hid_done = sem("up_silu"), sem("hid_done")
        hidhi, hidlo = sem("hidhi"), sem("hidlo")
        z_abs = sem("z_abs")
        z_out, z_exp, soft_rdy, soft_out = sem("z_out"), sem("z_exp"), sem("soft_rdy"), sem("soft_out")
        k_exp, k_rdy, s_log, s_cut, s_inv = sem("k_exp"), sem("k_rdy"), sem("s_log"), sem("s_cut"), sem("s_inv")
        ln_rdy, l_add, gates, o_ln = sem("ln_rdy"), sem("l_add"), sem("gates"), sem("o_ln")
        v_rdy, q_rdy, g_rdy = sem("v_rdy"), sem("q_rdy"), sem("g_rdy")
        c_exp, c_mul, c_tr, c_cp, st_mm, st_cp = (sem("c_exp"), sem("c_mul"), sem("c_tr"), sem("c_cp"),
                                                  sem("st_mm"), sem("st_cp"))
        dg_mm, dg_out = sem("dg_mm"), sem("dg_out")
        x_exp, x_mul, x_mm, x_cp = sem("x_exp"), sem("x_mul"), sem("x_mm"), sem("x_cp")
        l_sub, l_exp, l_mul, l_mm, l_cp = sem("l_sub"), sem("l_exp"), sem("l_mul"), sem("l_mm"), sem("l_cp")
        i_exp, i_mul, o_mm, o_cp, o_sq, o_sum = (sem("i_exp"), sem("i_mul"), sem("o_mm"), sem("o_cp"),
                                                 sem("o_sq"), sem("o_sum"))
        o_var, o_std, r32_done, rhi_done, rlo_done = (sem("o_var"), sem("o_std"), sem("r32_done"),
                                                      sem("rhi_done"), sem("rlo_done"))
        rt_hid, rt_rdy, lg_mm, tk_mm, tk_out = (sem("rt_hid"), sem("rt_rdy"), sem("lg_mm"), sem("tk_mm"),
                                                sem("tk_out"))
        rt_dif, rt_exp, pick, rk_mm, routed = sem("rt_dif"), sem("rt_exp"), sem("pick"), sem("rk_mm"), sem("routed")
        acc_rdy, oh_rdy, ga_mm, ga_hi, ga_lo = (sem("acc_rdy"), sem("oh_rdy"), sem("ga_mm"), sem("ga_hi"),
                                                sem("ga_lo"))
        sp_mm, sp_rdy = sem("sp_mm"), sem("sp_rdy")
        eu_silu, eu_hid, et_mm, et_hi, et_lo = (sem("eu_silu"), sem("eu_hid"), sem("et_mm"), sem("et_hi"),
                                                sem("et_lo"))
        ey32, ey_hi, ey_lo, sc_mm = sem("ey32"), sem("ey_hi"), sem("ey_lo"), sem("sc_mm")
        fin32, fin_tr, fin_out, stored = sem("fin32"), sem("fin_tr"), sem("fin_out"), sem("stored")

        block = es.enter_context(nc.Block())

        def slot(u):
            return u % R

        def fills(u):
            return u // R + 1

        def sel_bank(n, bank):
            return (2, 4)[n % 2] if bank == 0 else 6 + n % 2

        def base(g):
            return g % 2 * R_SET

        def heads(at, a=0, b=NT):
            return ar(at, HG * NT).rearrange("p (h t) -> p h t", h=HG)[:, :, a:b]

        def lat(at):
            return ar(at, G_LAT).rearrange("p (h t) -> p h t", h=HG)

        def temp(g, n):
            return temp2[:, :] if n % 2 == 0 else ar(base(g) + R_T, 2 * G_LAT)

        def gate_temp(g, d):
            return temp3[:, :] if d == 1 else ar(base(g) + R_T, HG * NT)

        def temp_lat(g, n, part):
            return temp(g, n)[:, part * G_LAT:(part + 1) * G_LAT].rearrange("p (h t) -> p h t", h=HG)

        def scores(g):
            at, step = base(g) + R_KF + N_LAT, R_KB - R_KF + P
            both = arena[:, at:at + 2 * step].rearrange("p (s x) -> p s x", s=2)[:, :, 0:HG * NT]
            return both.rearrange("p s (h t) -> p s h t", h=HG)[:, :, :, 0:P]

        def by_half(bank):
            return ps[:, bank, :].rearrange("p (s h t) -> p s h t", s=2, h=HG)

        def units_before(g, k):
            if g < NG - 1:
                return U_IN_ODD + G_UNITS * (g + 1) + k
            return U_OUT_ODD + (min(max(k - 2, 0), 6) if g == NG - 1 else 6)

        @block.sync
        def _(sp):
            def load(u, src, plus=0, looped=False):
                if looped or u >= R:
                    sp.wait_ge(lo_done, plus + (u - R + 1))
                sp.dma_start(raw[:, slot(u), :], src).then_inc(raw_in[slot(u)], 16)

            def cols(w, kt, n, col, width):
                return w[kt * P:(kt + n) * P, col:col + width].rearrange("(k p) c -> p k c", p=P)

            def load_cols(u, w, col, plus=0, looped=False):
                for k in range(4):
                    load(u + k, cols(w, 2 * k, 2, col, BANK), plus, looped)

            vr = ar(VEC_ROWS, P)
            for row, n, v in ((V_C, 8, c[0]), (V_CC, 8, c_ctx), (V_NMIX, 16, norm_mix), (V_NFFN, 16, norm_ffn),
                              (V_NOUT, 8, norm_out), (V_LB, 16, rec_lb[0]), (V_RNORM, 8, rec_norm[0])):
                flat = v if len(v.shape) == 1 else v.rearrange("a b -> (a b)")
                sp.dma_start(vr[row:row + n, :], flat.rearrange("(r q) -> r q", q=P)).then_inc(vec_in, 16)
            sp.dma_start(ar(B_ROWS, P)[0:96, :], b_ada.rearrange("l (r q) -> (l r) q", q=P)).then_inc(vec_in, 16)
            sp.dma_start(con[:, :], cst[:, 0:C_RES]).then_inc(con_in, 16)
            load_cols(U_ADA_A, w_ada[0], 0)
            for s, src in enumerate((x, ctx_in)):
                for t in range(LT):
                    sp.dma_start(ar(X_ROWS + (s * LT + t) * D, D), src[0, t * P:(t + 1) * P, :]).then_inc(x_in, 16)
            for b in range(1, 4):
                load_cols(U_ADA_A + 4 * b, w_ada[0], b * BANK)
            sp.dma_start(ar(MASK_F, C_MASK), msk).then_inc(mask_in, 16)
            sp.dma_start(ar(M_DFT, C_DFT), cst[:, C_RES:]).then_inc(mix_in, 16)
            sp.dma_start(ar(M_GW, B_H * P), gmlp_wt.rearrange("s h t -> s (h t)")).then_inc(mix_in, 16)
            sp.dma_start(gb_row, gmlp_b[0].rearrange("(a h) t -> a (h t)", a=1)).then_inc(mix_in, 16)
            for b in range(3):
                load_cols(U_IN_EVEN + 4 * b, w_in_even[0], b * BANK)
            for b in range(2):
                load_cols(U_ADA_C + 4 * b, w_ada[0], (4 + b) * BANK)
            for b in range(2):
                load_cols(U_OUT_EVEN + 4 * b, w_out_even[0], b * BANK)
            with sp.Fori(0, 2) as j:
                for b in range(3):
                    src = w_ada[0][:, bass.ds(j * (3 * BANK) + (6 + b) * BANK, BANK)]
                    for k in range(4):
                        load(U_ADA_E + 4 * b + k, src[2 * k * P:(2 * k + 2) * P, :].rearrange("(k p) c -> p k c", p=P),
                             plus=j * 12, looped=True)
            u = U_FFN
            for first, n in FF_HALF:
                for it in range(first, first + n):
                    for w in (ffn_w1[0], ffn_w3[0]):
                        for k in range(2):
                            load(u, cols(w, 4 * k, 4, it * FF_COLS, FF_COLS))
                            u += 1
                for ft in range(2 * first, 2 * (first + n)):
                    load(u, ffn_w2[0][ft * P:(ft + 1) * P, :])
                    u += 1
            with sp.Fori(0, 4) as j:
                for b in range(3):
                    src = w_ada[1][:, bass.ds(j * (3 * BANK) + b * BANK, BANK)]
                    for k in range(4):
                        load(U_ADA_G + 4 * b + k, src[2 * k * P:(2 * k + 2) * P, :].rearrange("(k p) c -> p k c", p=P),
                             plus=j * 12, looped=True)
            sp.dma_start(rt32[:, :].rearrange("p (k e) -> p k e", e=N_EXP),
                         router_w[0].rearrange("(k p) e -> p k e", p=P)).then_inc(rt_in, 16)
            u = U_IN_ODD
            for g in range(NG):
                for part in (2, 3, 4, 0, 1):
                    for k in range(2):
                        load(u, cols(w_in_odd[0], 4 * k, 4, part * R_W + g * HG * P, HG * P))
                        u += 1
            u = U_OUT_ODD
            for k in range(4):
                for b in range(2):
                    load(u, cols(w_out_odd[0], 2 * k, 2, b * BANK, BANK))
                    u += 1

            def expert_loads(e, past):
                def rows(w, kt, n):
                    m = w[0, bass.ds(e, 1), kt * P:(kt + n) * P, :]
                    return m.rearrange("a (k p) c -> p (a k) c", p=P)

                v = 0
                for cb in range(CB):
                    for w in (moe_w1, moe_w3):
                        for k in range(4):
                            load(U_MOE + v, rows(w, 2 * k, 2)[:, :, cb * BANK:(cb + 1) * BANK], past, looped=True)
                            v += 1
                for kt in range(EXP_KT):
                    load(U_MOE + v, rows(moe_w2, kt, 1), past, looped=True)
                    v += 1

            with sp.Fori(0, N_EXP) as e:
                expert_loads(e, e * EXP_UNITS)
            sp.wait_ge(routed, 1)
            n_over = sp.value_load(trips[0:1, T_OVER:T_OVER + 1], min_val=0, max_val=N_OVER)
            n_past = sp.value_load(trips[0:1, 0:1], min_val=N_EXP, max_val=TURNS)
            with sp.If(n_over):
                with sp.Fori(0, n_over) as j:
                    e = sp.value_load(trips[0:1, bass.ds(j + T_EXPERT, 1)], min_val=0, max_val=N_EXP - 1)
                    expert_loads(e, j * EXP_UNITS + N_EXP * EXP_UNITS)
                sp.nop()
            for k in range(LEAD):
                load(U_MOE + k, cols(moe_w1[0, 0], 2 * (k % 4), 2, 0, BANK), n_past * EXP_UNITS, looped=True)

            for t in range(LT):
                sp.wait_ge(fin_out, t + 1)
                sp.dma_start(out[0, t * P:(t + 1) * P, :], ar(X_OUT + t * D, D)).then_inc(stored, 16)
            sp.wait_ge(stored, 16 * LT)

        @block.tensor
        def _(pe):
            def three(dst, s_h, s_l, m_h, m_l, start, stop, **kw):
                pe.matmul(dst, s_h, m_h, start=start, stop=False, **kw)
                pe.matmul(dst, s_l, m_h, start=False, stop=False, **kw)
                return pe.matmul(dst, s_h, m_l, start=False, stop=stop, **kw)

            def unit(u, plus=0):
                pe.wait_ge(lo_done, plus + (u + 1))
                return w_hi[:, slot(u), :], w_lo[:, slot(u), :]

            def ada_sel_mm(n, bank, after):
                pe.wait_ge(ada_row, after + 1)
                if not isinstance(after, int):
                    pe.wait_ge(ada_done, after)
                elif after >= 2:
                    pe.wait_ge(ada_done, after - 1)
                for q in range(4):
                    m = pe.matmul(ps[:, sel_bank(n, bank), 2 * q:2 * q + 2],
                                  ar(ADA_ROW + n % 2 * BANK, BANK)[0:4, q * P:(q + 1) * P],
                                  con[0:4, C_SEL:C_SEL + 2], start=True, stop=True)
                m.then_inc(ada_sel, 1)

            def ada_block(n, u, bank, plus=0):
                b = n % 2
                for k in range(4):
                    hi, lo = unit(u + k, plus)
                    for kk in range(2):
                        kt = 2 * k + kk
                        st = cond[:, kt * 4:kt * 4 + P]
                        pe.matmul(ps[:, bank + b, :], st, hi[:, kk * BANK:(kk + 1) * BANK],
                                  start=(kt == 0), stop=False)
                        m = pe.matmul(ps[:, bank + b, :], st, lo[:, kk * BANK:(kk + 1) * BANK],
                                      start=False, stop=(kt == KT - 1))
                    m.then_inc(pe_used, 1)

            def ada_blocks(n0, count, u, bank):
                for n in range(n0, n0 + count):
                    if n - n0 >= 2:
                        pe.wait_ge(ada_row, n - 1)
                    ada_block(n, u + 4 * (n - n0), bank)
                    if n > n0:
                        ada_sel_mm(n - 1, bank, n - 1)
                ada_sel_mm(n0 + count - 1, bank, n0 + count - 1)

            def norm_sum(n, width):
                if 0 < n < 4:
                    pe.wait_ge(resid, RESID_AT[n] + (4 if n < 3 else KT))
                for kt in range(KT):
                    pe.wait_ge(sq_done, KT * n + kt + 1)
                    pe.matmul(ps[:, 3, 0:width], ones, ar(NORM_AT[n] + kt % 2 * NT, width),
                              start=(kt == 0), stop=(kt == KT - 1)).then_inc(sq_mm, 1)

            pe.wait_ge(con_in, 16)
            pe.wait_ge(vec_in, 16 * 8)
            pe.transpose(ps[:, 0, 0:V_ROWS], ar(VEC_ROWS, P)[0:V_ROWS, :], con[0:V_ROWS, C_ID:C_ID + V_ROWS])
            pe.transpose(ps[:, 0, 128:224], ar(B_ROWS, P)[0:96, :], con[0:96, C_ID:C_ID + 96]).then_inc(vec_tr, 1)
            pe.wait_ge(x_in, 16 * TT)
            for kt in range(KT):
                if kt == KT - 1:
                    pe.wait_ge(vec_out, 2)
                for t in range(TT):
                    m = pe.transpose(ps[:, (1 + kt) % 8, t * P:(t + 1) * P],
                                     ar(X_ROWS + t * D + kt * P, P), ident)
                m.then_inc(x_tr, 1)

            pe.wait_ge(cond_rdy, 1)
            pe.wait_ge(x_out, 8)
            norm_sum(0, NT)
            ada_blocks(0, 4, U_ADA_A, 0)

            u = U_IN_EVEN
            pe.wait_ge(ada_done, 4)
            for blk, bank in ((0, 0), (1, 4)):
                for k in range(4):
                    hi, lo = unit(u)
                    for kk in range(2):
                        kt = 2 * k + kk
                        if blk == 0:
                            pe.wait_ge(h_done, kt + 1)
                        for n in range(4):
                            a, b = kk * BANK + n * P, kk * BANK + (n + 1) * P
                            m = three(ps[:, bank + n, :], hi[:, a:b], lo[:, a:b], hh(kt), hl(kt), kt == 0, kt == KT - 1)
                    m.then_inc(pe_used, 1)
                    u += 1
            pe.wait_ge(a_out, 4)
            for k in range(4):
                hi, lo = unit(u)
                for kk in range(2):
                    kt = 2 * k + kk
                    for t in range(TT):
                        a, b = t * P, (t + 1) * P
                        m = three(ps[:, t, :], hh(kt, a, b), hl(kt, a, b), hi[:, kk * BANK:(kk + 1) * BANK],
                                  lo[:, kk * BANK:(kk + 1) * BANK], kt == 0, kt == KT - 1)
                m.then_inc(pe_used, 1)
                u += 1

            pe.wait_ge(u_out, 4)
            ada_blocks(4, 2, U_ADA_C, 4)

            pe.wait_ge(mix_in, 48)
            n = 0
            for g in range(A_G):
                for tp in range(2):
                    if n == 0:
                        pe.wait_ge(v_out, 4)
                    if n == 4:
                        pe.wait_ge(ada_done, 6)
                    for q in range(2):
                        t = 2 * tp + q
                        m = pe.matmul(ps[:, n, q * 256:(q + 1) * 256], ar(M_A + g * NT + t * P, P),
                                      ar(M_DFT + DFT_CS, 256), start=True, stop=True)
                    m.then_inc(dft_mm, 1)
                    n += 1
            acs = ar(M_ACS, TT * A_G * 256).rearrange("p (t g c) -> p t g c", t=TT, g=A_G)
            for g in range(A_G):
                pe.wait_ge(dft_out, 2 * (g + 1))
                for s in range(2):
                    for t in range(LT):
                        tok = s * LT + t
                        pe.matmul(ps[:, g, s * 256:(s + 1) * 256], acs[:, tok, g, 0:P],
                                  ar(M_DFT + DFT_CT + t * N_LAT, N_LAT), start=(t == 0), stop=False)
                        m = pe.matmul(ps[:, g, s * 256:(s + 1) * 256], acs[:, tok, g, P:2 * P],
                                      ar(M_DFT + DFT_ST + t * N_LAT, N_LAT), start=False, stop=(t == LT - 1))
                m.then_inc(y_mm, 1)
            pe.wait_ge(dft_out, 8)
            pe.wait_ge(ln_done, 16)
            for h in range(B_H):
                for t in range(TT):
                    m = pe.matmul(ps[:, 4 + h, t * P:(t + 1) * P], ar(M_V + t * BANK + h * P, P),
                                  ar(M_GW + h * P, P), start=(t == 0), stop=False, skip_group_check=True)
                    m = pe.matmul(ps[:, 4 + h, t * P:(t + 1) * P], con[32:33, C_ONE:C_ONE + P],
                                  gb_row[:, h * P:(h + 1) * P], start=False, stop=(t == TT - 1),
                                  skip_group_check=True)
                m.then_inc(y_mm, 1)

            u = U_OUT_EVEN
            for blk in range(2):
                bank = 4 * blk
                for k in range(4):
                    hi, lo = unit(u)
                    for kk in range(2):
                        kt = 2 * k + kk
                        if blk == 0:
                            pe.wait_ge(ylo_done, kt + 1 if kt >= 4 else 4)
                        else:
                            pe.wait_ge(ylo_done, 8)
                        for n in range(4):
                            a, b = kk * BANK + n * P, kk * BANK + (n + 1) * P
                            m = three(ps[:, bank + n, :], hi[:, a:b], lo[:, a:b], hh(kt), hl(kt), kt == 0, kt == KT - 1)
                    m.then_inc(pe_used, 1)
                    u += 1

            norm_sum(1, NT)
            pe.wait_ge(resid, 8)
            with pe.Fori(0, 2) as j:
                for n in range(3):
                    ada_block(n, U_ADA_E + 4 * n, 0, plus=j * 12)
                    ada_sel_mm(n, 0, j * 3 + 6 + n)

            u = U_FFN
            for half, (first, count) in enumerate(FF_HALF):
                for it in range(first, first + count):
                    bank = 4 * (it % 2)
                    if it == 0:
                        pe.wait_ge(ada_done, 12)
                    if half == 1 and it < first + 2:
                        pe.wait_ge(resid, (12, 16)[it % 2])
                    elif it >= 2:
                        pe.wait_ge(hid_done, it - 1)
                    for w in range(2):
                        for k in range(2):
                            hi, lo = unit(u)
                            for kk in range(4):
                                kt = 4 * k + kk
                                if it == 0 and w == 0:
                                    pe.wait_ge(h_done, KT + kt + 1)
                                for n in range(2):
                                    a, b = kk * FF_COLS + n * P, kk * FF_COLS + (n + 1) * P
                                    m = three(ps[:, bank + 2 * w + n, :], hi[:, a:b], lo[:, a:b], hh(kt), hl(kt),
                                              kt == 0, kt == KT - 1)
                            m.then_inc(pe_used, 1)
                            u += 1
                last = first + count - 1
                order = [(n + 4 * ((last + 1) % 2)) % KT for n in range(KT)]
                pe.wait_ge(hid_done, last)
                for f in range(2 * count):
                    pe.wait_ge(hidlo, 2 * first + f + 1)
                    hi, lo = unit(u)
                    sl = f % 6 * NT
                    for n in order:
                        if f == 0 and n == order[4]:
                            pe.wait_ge(hid_done, last + 1)
                        m = three(ps[:, n, :], hi[:, n * P:(n + 1) * P], lo[:, n * P:(n + 1) * P],
                                  s_hi[:, sl:sl + NT], s_lo[:, sl:sl + NT], f == 0, f == 2 * count - 1)
                    m.then_inc(pe_used, 1)
                    u += 1

            norm_sum(2, NT)
            pe.wait_ge(resid, 24)
            with pe.Fori(0, 4) as j:
                for n in range(3):
                    ada_block(n, U_ADA_G + 4 * n, 0, plus=j * 12)
                    ada_sel_mm(n, 0, j * 3 + 12 + n)

            def project(g, k):
                part, half = k // 2, k % 2
                if half == 0:
                    if part == 0 and g > 0:
                        pe.wait_ge(v_rdy, g)
                    if part == 1 and g > 0:
                        pe.wait_ge(g_rdy, g)
                    if part == 2:
                        pe.wait_ge(z_out, 2 * g + 1)
                    if part == 3:
                        pe.wait_ge(z_out, 2 * g + 2)
                hi, lo = unit(U_IN_ODD + G_UNITS * g + k)
                for kk in range(4):
                    kt = 4 * half + kk
                    if g == 0 and part == 0:
                        pe.wait_ge(h_done, 2 * KT + kt + 1)
                    if part == 2:
                        for t in range(TT):
                            a, b, c = t * P, (t + 1) * P, kk * HG * P
                            m = three(ps[:, t // 2, t % 2 * 256:t % 2 * 256 + 256], hh(kt, a, b), hl(kt, a, b),
                                      hi[:, c:c + HG * P], lo[:, c:c + HG * P], kt == 0 and t % 2 == 0,
                                      kt == KT - 1 and t % 2 == 1, skip_group_check=True)
                        continue
                    for n in range(HG):
                        a, b = (kk * HG + n) * P, (kk * HG + n + 1) * P
                        if part < 2:
                            m = three(ps[:, 2 * part + n, :], hi[:, a:b], lo[:, a:b], hh(kt), hl(kt),
                                      kt == 0, kt == KT - 1)
                        else:
                            m = three(ps[:, part - 1, n * 256:(n + 1) * 256], hi[:, a:b], lo[:, a:b],
                                      hh(kt, 0, N_LAT), hl(kt, 0, N_LAT), kt == 0 and n == 0,
                                      kt == KT - 1 and n == HG - 1, skip_group_check=True)
                m.then_inc(pe_used, 1)

            def out_odd(k, blk):
                hi, lo = unit(U_OUT_ODD + 2 * k + blk)
                pe.wait_ge(rlo_done, 2 * k + 2)
                if k == 0 and blk == 0:
                    pe.wait_ge(g_rdy, NG)
                for kk in range(2):
                    kt = 2 * k + kk
                    for n in range(4):
                        a, b = kk * BANK + n * P, kk * BANK + (n + 1) * P
                        dst = ps[:, 2 * blk + n // 2, n % 2 * 256:n % 2 * 256 + 256]
                        m = three(dst, hi[:, a:b], lo[:, a:b], s_hi[:, kt * N_LAT:(kt + 1) * N_LAT],
                                  s_lo[:, kt * N_LAT:(kt + 1) * N_LAT], kt == 0 and n % 2 == 0,
                                  kt == KT - 1 and n % 2 == 1, skip_group_check=True)
                m.then_inc(pe_used, 1)

            def level(g, n):
                pe.wait_ge(l_mul, len(LEVELS) * g + n + 1)
                if n == 0:
                    if g > 0:
                        pe.wait_ge(o_var, g)
                elif n == 1:
                    pe.wait_ge(dg_out, g + 1)
                else:
                    pe.wait_ge(l_cp, len(LEVELS) * g + n - 1)
                keys, queries = temp_lat(g, n, 0), temp_lat(g, n, 1)
                for seg in range(2):
                    for h in range(HG):
                        a, b = seg * P, (seg + 1) * P
                        m = pe.matmul(ps[:, 6 - n % 2, (seg * HG + h) * P:(seg * HG + h + 1) * P],
                                      keys[:, h, a:b], queries[:, h, a:b], start=True, stop=True)
                m.then_inc(l_mm, 1)

            def turned_keys(g):
                for d in range(2):
                    pe.wait_ge(c_mul, 2 * g + d + 1)
                    if d == 0 and g > 0:
                        pe.wait_ge(x_cp, g)
                    if d == 1 and g > 0:
                        pe.wait_ge(l_cp, len(LEVELS) * g - 1)
                    kbuf = heads(base(g) + (R_KF, R_KB)[d], N_LAT, NT)
                    for seg in range(2):
                        for h in range(HG):
                            m = pe.transpose(ps[:, 4 + d, (seg * HG + h) * P:(seg * HG + h + 1) * P],
                                             kbuf[:, h, seg * P:(seg + 1) * P], ident)
                    m.then_inc(c_tr, 1)

            def outputs(g):
                pe.wait_ge(l_cp, len(LEVELS) * (g + 1))
                pe.wait_ge(i_mul, g + 1)
                b = base(g)
                s0, s1 = heads(b + R_KF, N_LAT, NT), heads(b + R_KB, N_LAT, NT)
                sf, sb_ = heads(b + R_LF, N_LAT, N_LAT + P), heads(b + R_LB, N_LAT, N_LAT + P)
                for h in range(HG):
                    dst = ps[:, 7, h * 256:(h + 1) * 256]
                    pe.matmul(dst, ar(b + R_V + h * P, P), s0[:, h, :], start=True, stop=False)
                    pe.matmul(dst, ar(b + R_V + HG * P + h * P, P), s1[:, h, :], start=False, stop=False)
                    pe.matmul(dst, sf[:, h, :], temp_lat(g, 1, 0)[:, h, :], start=False, stop=False)
                    m = pe.matmul(dst, sb_[:, h, :], temp_lat(g, 1, 1)[:, h, :], start=False, stop=True)
                m.then_inc(o_mm, 1)

            def states(g):
                pe.wait_ge(c_cp, 2 * g + 2)
                for d in range(2):
                    kt_ = temp(g, 1)[:, d * 2 * HG * P:(d + 1) * 2 * HG * P].rearrange("p (s h c) -> p s h c", s=2, h=HG)
                    for h in range(HG):
                        for seg in range(2):
                            m = pe.matmul(ps[:, 4, (d * HG + h) * P:(d * HG + h + 1) * P], kt_[:, seg, h, :],
                                          ar(base(g) + R_V + (2 + seg) * HG * P + h * P, P),
                                          start=(seg == 0), stop=(seg == 1))
                m.then_inc(st_mm, 1)

            def diagonal(g):
                pe.wait_ge(q_rdy, g + 1)
                b = base(g)
                kf, kb, q = heads(b + R_KF, 0, N_LAT), heads(b + R_KB, 0, N_LAT), lat(b + R_Q)
                for seg in range(2):
                    for h in range(HG):
                        dst = ps[:, 5, (seg * HG + h) * P:(seg * HG + h + 1) * P]
                        a = slice(seg * P, (seg + 1) * P)
                        pe.matmul(dst, kf[:, h, a], q[:, h, a], start=True, stop=False)
                        m = pe.matmul(dst, kb[:, h, a], q[:, h, a], start=False, stop=True)
                m.then_inc(dg_mm, 1)

            def cross(g):
                pe.wait_ge(x_mul, g + 1)
                pe.wait_ge(st_cp, g + 1)
                keys, queries = temp_lat(g, 1, 0), temp_lat(g, 1, 1)
                for d in range(2):
                    a, b = slice(d * P, (d + 1) * P), slice((1 - d) * P, (2 - d) * P)
                    for h in range(HG):
                        m = pe.matmul(ps[:, 4, (d * HG + h) * P:(d * HG + h + 1) * P], keys[:, h, a],
                                      queries[:, h, b], start=True, stop=True)
                m.then_inc(x_mm, 1)

            for g in range(-1, NG + 1):
                for k in range(G_UNITS):
                    if k == 0 and g > 0:
                        level(g - 1, 6)
                    if k == 0 and 0 <= g < NG:
                        turned_keys(g)
                    if k == 1 and g > 0:
                        outputs(g - 1)
                    if k == 1 and 0 <= g < NG:
                        states(g)
                    if k == 2 and 0 <= g < NG:
                        diagonal(g)
                    if k == 2 and g > 0:
                        pe.wait_ge(o_sq, g)
                        pe.matmul(ps[:, 6, :], ones, temp(g - 1, 1)[:, G_LAT:], start=True, stop=True).then_inc(o_sum, 1)
                    if k == 3 and 0 <= g < NG:
                        cross(g)
                    if k >= 4 and 0 <= g < NG:
                        level(g, k - 4)
                    if g == -1:
                        if k == 0:
                            pe.wait_ge(ada_done, 24)
                        project(0, k)
                    elif g < NG - 1:
                        project(g + 1, k)
                    elif g == NG - 1 and 2 <= k < 8:
                        out_odd((k - 2) // 2, k % 2)
            out_odd(3, 0)
            out_odd(3, 1)
            norm_sum(3, N_LAT)

            pe.wait_ge(rt_rdy, 1)
            for kt in range(KT):
                pe.wait_ge(h_done, 3 * KT + kt + 1)
                for t in range(LT):
                    m = three(ps[:, 2 * t, 0:N_EXP], hh(kt, t * P, (t + 1) * P), hl(kt, t * P, (t + 1) * P),
                              rt_hi[:, kt * N_EXP:(kt + 1) * N_EXP], rt_lo[:, kt * N_EXP:(kt + 1) * N_EXP],
                              kt == 0, kt == KT - 1)
            m.then_inc(lg_mm, 1)
            n = 0
            for part in (h_hi, h_lo):
                for t in range(LT):
                    for kq in range(2):
                        if n >= 4:
                            pe.wait_ge(tk_out, n - 3)
                        for k in range(4):
                            kt = 4 * kq + k
                            m = pe.transpose(ps[:, 4 + n % 4, k * P:(k + 1) * P],
                                             part[:, kt * NT + t * P:kt * NT + (t + 1) * P].bitcast(F32), ident)
                        m.then_inc(tk_mm, 1)
                        n += 1
            pe.wait_ge(pick, 1)
            pe.matmul(ps[:, 1, 0:8], tri, route[:, 0, 32:40], start=True, stop=True)
            pe.matmul(ps[:, 1, 8:16], tri, route[:, 1, 32:40], start=True, stop=False)
            pe.matmul(ps[:, 1, 8:16], ones, route[:, 0, 32:40], start=False, stop=True)
            pe.matmul(ps[:, 1, 16:24], ones, route[:, 0, 32:40], start=True, stop=False)
            pe.matmul(ps[:, 1, 16:24], ones, route[:, 1, 32:40], start=False, stop=True).then_inc(rk_mm, 1)

            def gather():
                for q, part in enumerate((s_hi, s_lo)):
                    for kt in range(KT):
                        for t in range(LT):
                            m = pe.matmul(ps[:, 2 * q + kt // 4, kt % 4 * P:(kt % 4 + 1) * P],
                                          part[:, t * D + kt * P:t * D + (kt + 1) * P], onehot[:, t, :],
                                          start=(t == 0), stop=(t == LT - 1))
                return m

            def turn_hidden(i, cb):
                pe.wait_ge(eu_hid, i * CB + (cb + 1))
                if cb == 0:
                    pe.wait_ge(acc_rdy, i * 2 + 3)
                else:
                    pe.wait_ge(et_lo, i * CB + cb)
                for q in range(4):
                    m = pe.transpose(ps[:, 6, q * P:(q + 1) * P], ar(X_HID + q * P, P), ident)
                m.then_inc(et_mm, 1)

            def scatter(i, half):
                pe.wait_ge(ey_lo, i * 2 + (half + 1))
                if half == 0:
                    pe.wait_ge(sp_rdy, i + 1)
                else:
                    pe.wait_ge(acc_rdy, i * 2 + 2)
                yh, yl = y_parts(half)
                for n in range(4):
                    dst = ps[:, 6 + n // 2, n % 2 * 256:n % 2 * 256 + 256]
                    pe.matmul(dst, yh[:, n * P:(n + 1) * P], spread[:, :], start=True, stop=False)
                    m = pe.matmul(dst, yl[:, n * P:(n + 1) * P], spread[:, :], start=False, stop=True)
                m.then_inc(sc_mm, 1)

            pe.wait_ge(oh_rdy, 1)
            pe.wait_ge(tk_out, 8)
            gather().then_inc(ga_mm, 1)
            n_turns = pe.value_load(trips[0:1, 0:1], min_val=N_EXP, max_val=TURNS)
            with pe.Fori(0, n_turns) as i:
                past = i * EXP_UNITS
                pe.wait_ge(ga_lo, i + 1)
                v = 0
                for cb in range(CB):
                    bank = 2 * (cb % 2)
                    if cb >= 2:
                        pe.wait_ge(eu_hid, i * CB + (cb - 1))
                    for w in range(2):
                        for k in range(4):
                            hi, lo = unit(U_MOE + v, past)
                            for kk in range(2):
                                kt = 2 * k + kk
                                g = slice(2048 + kt * P, 2048 + (kt + 1) * P)
                                m = three(ps[:, bank + w, :], s_hi[:, g], s_lo[:, g], hi[:, kk * BANK:(kk + 1) * BANK],
                                          lo[:, kk * BANK:(kk + 1) * BANK], kt == 0, kt == KT - 1)
                            m.then_inc(pe_used, 1)
                            v += 1
                            if v == 8:
                                scatter(i, 0)
                            if v == 11:
                                scatter(i, 1)
                        if w == 0 and cb >= 1:
                            turn_hidden(i, cb - 1)
                    if cb == 2:
                        for t in range(LT):
                            pe.transpose(ps[:, 7, t * P:(t + 1) * P], onehot[:, t, :].bitcast(F32), ident)
                        for t in range(LT):
                            m = pe.matmul(ps[:, 7, 256:257], onehot[:, t, :].bitcast(F32), cw[:, t:t + 1],
                                          start=(t == 0), stop=(t == LT - 1))
                        m.then_inc(sp_mm, 1)
                pe.wait_ge(ey32, i + 1)
                for kt in range(EXP_KT):
                    if kt % 4 == 0:
                        pe.wait_ge(et_lo, i * CB + (kt // 4 + 1))
                    hi, lo = unit(U_MOE + v, past)
                    for n in range(2):
                        m = three(ps[:, 4 + n, :], h_hi[:, kt * P:(kt + 1) * P], h_lo[:, kt * P:(kt + 1) * P],
                                  hi[:, n * BANK:(n + 1) * BANK], lo[:, n * BANK:(n + 1) * BANK],
                                  kt == 0, kt == EXP_KT - 1)
                    m.then_inc(pe_used, 1)
                    v += 1
                    if kt == 3:
                        turn_hidden(i, CB - 1)
                    if kt == 11:
                        pe.wait_ge(oh_rdy, i + 2)
                        gather().then_inc(ga_mm, 1)
            scatter(n_turns, 0)
            scatter(n_turns, 1)

            norm_sum(4, N_LAT)
            for n in range(4):
                for kt in (range(4), range(4, 8))[n % 2]:
                    pe.wait_ge(fin32, kt + 1)
                    t = n // 2
                    m = pe.transpose(ps[:, 4 + n, kt % 4 * P:(kt % 4 + 1) * P], xT[:, kt, t * P:(t + 1) * P], ident)
                m.then_inc(fin_tr, 1)

        @block.gpsimd
        def _(pool):
            pool.wait_ge(mask_in, 16)
            pool.tensor_copy(masks[:, :], ar(MASK_F, C_MASK)).then_inc(mask_rdy, 1)

            def blocks(view, hs):
                return view.rearrange("p h (b c) -> p h b c", c=2 * hs)

            def level_sub(g, n):
                if n == 0:
                    pool.wait_ge(gates, 2 * g + 2)
                    if g > 0:
                        pool.wait_ge(l_mm, len(LEVELS) * g)
                elif n == 1:
                    pool.wait_ge(x_mm, g + 1)
                else:
                    pool.wait_ge(l_mm, len(LEVELS) * g + n - 1)
                hs, nb = LEVELS[n], N_LAT // (2 * LEVELS[n])
                keys, queries = (blocks(temp_lat(g, n, k), hs) for k in range(2))
                lf, lbk = (blocks(heads(base(g) + a, 0, N_LAT), hs) for a in (R_LF, R_LB))
                ref_f = lf[:, :, :, hs - 1:hs].broadcast_to([P, HG, nb, hs])
                ref_b = lbk[:, :, :, hs:hs + 1].broadcast_to([P, HG, nb, hs])
                pool.tensor_tensor(keys[:, :, :, 0:hs], ref_f, lf[:, :, :, 0:hs], ALU.subtract)
                pool.tensor_tensor(keys[:, :, :, hs:], lbk[:, :, :, hs:], ref_b, ALU.subtract)
                pool.tensor_tensor(queries[:, :, :, 0:hs], ref_b, lbk[:, :, :, 0:hs], ALU.subtract)
                pool.tensor_tensor(queries[:, :, :, hs:], lf[:, :, :, hs:], ref_f, ALU.subtract).then_inc(l_sub, 1)

            def gate_add(p, d):
                t, lfl = gate_temp(p, d), ar(base(p) + (R_LF, R_LB)[d], HG * NT)
                pool.wait_ge(ln_rdy, 2 * p + d + 1)
                pool.tensor_tensor(t, t, lfl, ALU.add).then_inc(l_add, 1)

            for g in range(-1, NG):
                p, rec, proj = g + 1, g >= 0, g < NG - 1
                for k in range(3, G_UNITS):
                    if rec:
                        level_sub(g, k - 3)
                    if proj and k == 8:
                        gate_add(p, 1)
            pool.wait_ge(rlo_done, HEADS)
            pool.memset(ar(X_ACC, KT * N_LAT), 0.0).then_inc(acc_rdy, 1)

        @block.scalar
        def _(act):
            split = [0]

            def hi(u, turn=0, per=0):
                act.wait_ge(raw_in[slot(u)], turn * (per // R * 16) + 16 * fills(u))
                if per or u >= R:
                    act.wait_ge(pe_used, turn * per + (u - R + 1))
                act.activation(w_hi[:, slot(u), :], raw[:, slot(u), :], ACT.Copy).then_inc(hi_done, 1)

            def split_to(n):
                while split[0] < n:
                    hi(split[0])
                    split[0] += 1

            def ada_rows(n, bank):
                act.wait_ge(pe_used, 4 * (n + 1) if n < 4 else U_ADA_C + 4 * (n - 3))
                if n >= 2:
                    act.wait_ge(ada_sel, n - 1)
                act.activation(ar(ADA_ROW + n % 2 * BANK, BANK)[0:4, :], ps[0:4, bank + n % 2, :],
                               ACT.Copy).then_inc(ada_row, 1)

            def squares(n, width):
                for kt in range(KT):
                    if n > 0:
                        act.wait_ge(resid, RESID_AT[n] + kt + 1)
                    if n > 0 or kt >= 2:
                        act.wait_ge(sq_mm, KT * n + kt - 1)
                    act.activation(ar(NORM_AT[n] + kt % 2 * NT, width), xT[:, kt, 0:width],
                                   ACT.Square).then_inc(sq_done, 1)

            def norm_std(n, width):
                act.wait_ge(var_done, n + 1)
                act.activation(ar(NORM_AT[n] + 2 * NT, width), ar(NORM_AT[n] + 2 * NT, width),
                               ACT.Sqrt).then_inc(std_done, 1)

            def norm_hi(n, width):
                for kt in range(KT):
                    act.wait_ge(h32_done, KT * n + kt + 1)
                    act.activation(hh(kt, 0, width), ar(NORM_AT[n] + (3 + kt % 4) * NT, width),
                                   ACT.Copy).then_inc(hhi_done, 1)

            act.wait_ge(vec_out, 2)
            act.activation(sil[:, :], vT[:, V_C:V_C + 16], ACT.Silu).then_inc(silu_c, 1)
            act.wait_ge(silu_c, 1)
            cv = cond[:, 0:KT * 4].rearrange("p (k s) -> p s k", s=4)
            for s in range(2):
                act.activation(cv[:, s, :], sil[:, s * KT:(s + 1) * KT], ACT.Copy).then_inc(cond_hi, 1)
            act.wait_ge(lb_dif, 1)
            act.activation(lb[:, :], lb[:, :], ACT.Exp).then_inc(lb_exp, 1)
            split_to(R - 1)
            for kt in range(KT):
                act.wait_ge(x_tr, kt + 1)
                act.activation(xT[:, kt, :], ps[:, (1 + kt) % 8, :], ACT.Copy).then_inc(x_out, 1)
            act.wait_ge(x_out, 8)
            squares(0, NT)
            norm_std(0, NT)

            for n in range(4):
                split_to(4 * n + 4 + LEAD)
                ada_rows(n, 0)
            norm_hi(0, NT)
            split_to(U_IN_EVEN + 8 + LEAD)
            act.wait_ge(pe_used, U_IN_EVEN + 8)
            for n in range(4):
                act.activation(ar(M_U + n * NT, NT), ps[:, 4 + n, :], ACT.Gelu).then_inc(u_out, 1)
            split_to(U_IN_EVEN + 12 + LEAD)
            act.wait_ge(pe_used, U_IN_EVEN + 12)
            act.wait_ge(mask_rdy, 1)
            for n in range(4):
                act.activation(ar(M_V + n * BANK, BANK), ps[:, n, :], ACT.Gelu).then_inc(v_out, 1)
            for n in range(4, 6):
                split_to(U_ADA_C + 4 * (n - 3) + LEAD)
                ada_rows(n, 4)
            act.wait_ge(lnv, 1)
            act.activation(rs[:, :], rs[:, :], ACT.Sqrt).then_inc(lns, 1)
            for n in range(8):
                act.wait_ge(dft_mm, n + 1)
                g, tp = n // 2, n % 2
                acs = ar(M_ACS, TT * A_G * 256).rearrange("p (t g c) -> p t g c", t=TT, g=A_G)
                act.activation(acs[:, 2 * tp:2 * tp + 2, g, :], ps[:, n, :].rearrange("p (t c) -> p t c", t=2),
                               ACT.Copy).then_inc(dft_out, 1)
            for g in range(4):
                act.wait_ge(y_mm, g + 1)
                act.activation(hh(g), ps[:, g, :], ACT.Copy).then_inc(yhi_done, 1)
            for h in range(4):
                act.wait_ge(y32_done, h + 1)
                act.activation(hh(4 + h), ar(M_TMP + h % 2 * NT, NT), ACT.Copy).then_inc(yhi_done, 1)
            split_to(U_OUT_EVEN + 8 + LEAD)
            squares(1, NT)
            norm_std(1, NT)
            with act.Fori(0, 2) as j:
                for n in range(3):
                    for k in range(4):
                        hi(U_ADA_E + LEAD + 4 * n + k, j, 12)
                    act.wait_ge(pe_used, j * 12 + (U_ADA_E + 4 * (n + 1)))
                    act.wait_ge(ada_sel, j * 3 + (6 + n))
                    act.activation(ar(ADA_ROW + n % 2 * BANK, BANK)[0:4, :], ps[0:4, n % 2, :],
                                   ACT.Copy).then_inc(ada_row, 1)
            split[0] = U_FFN + LEAD
            norm_hi(1, NT)
            def hidden_hi(f, slot_free=0):
                if slot_free:
                    act.wait_ge(pe_used, slot_free)
                act.activation(s_hi[:, f % 6 * NT:(f % 6 + 1) * NT], ar(F_HID + f * NT, NT), ACT.Copy).then_inc(hidhi, 1)

            u = U_FFN
            for first, count in FF_HALF:
                for it in range(first, first + count):
                    if it == first + count - 1:
                        act.wait_ge(hid_done, first + 2)
                        for f in range(4):
                            hidden_hi(f)
                    u += 4
                    split_to(u + LEAD)
                    act.wait_ge(pe_used, u)
                    if it >= 2:
                        act.wait_ge(hid_done, it - 1)
                    act.activation(ar(F_SIL + it % 2 * 1024, 1024), ps[:, 4 * (it % 2):4 * (it % 2) + 2, :],
                                   ACT.Silu).then_inc(up_silu, 1)
                act.wait_ge(hid_done, first + count)
                for f in range(2 * count):
                    if f >= 4:
                        hidden_hi(f, u + f - 6 + 1 if f >= 6 else 0)
                    split_to(u + f + LEAD)
                u += 2 * count
            split_to(U_ADA_G + LEAD)
            squares(2, NT)
            norm_std(2, NT)
            with act.Fori(0, 4) as j:
                for n in range(3):
                    for k in range(4):
                        hi(U_ADA_G + LEAD + 4 * n + k, j, 12)
                    act.wait_ge(pe_used, j * 12 + (U_ADA_G + 4 * (n + 1)))
                    act.wait_ge(ada_sel, j * 3 + (12 + n))
                    act.activation(ar(ADA_ROW + n % 2 * BANK, BANK)[0:4, :], ps[0:4, n % 2, :],
                                   ACT.Copy).then_inc(ada_row, 1)
            split[0] = U_IN_ODD + LEAD
            norm_hi(2, NT)

            def gate_soft(p):
                for d in range(2):
                    act.wait_ge(z_abs, 2 * p + d + 1)
                    act.activation(gate_temp(p, d), gate_temp(p, d), ACT.Exp).then_inc(z_exp, 1)
                for d in range(2):
                    act.wait_ge(z_exp, 2 * p + d + 1)
                    act.activation(gate_temp(p, d), gate_temp(p, d), ACT.Ln, bias=1.0).then_inc(soft_rdy, 1)

            def gate_k(p, d):
                act.wait_ge(soft_out, 2 * p + d + 1)
                kk = ar(base(p) + (R_KF, R_KB)[d], HG * NT)
                act.activation(kk, kk, ACT.Exp, scale=-1.0).then_inc(k_exp, 1)

            def gate_bound(p):
                for d in range(2):
                    act.wait_ge(s_cut, 2 * p + d + 1)
                    act.activation(gate_temp(p, d), gate_temp(p, d), ACT.Exp, scale=-1.0).then_inc(s_inv, 1)
                for d in range(2):
                    act.wait_ge(s_inv, 2 * p + d + 1)
                    for h in range(HG):
                        col = d * HEADS + p * HG + h
                        th = gate_temp(p, d)[:, h * NT:(h + 1) * NT]
                        m = act.activation(th, th, ACT.Ln, bias=1.0, scale=lb[:, col:col + 1])
                    m.then_inc(ln_rdy, 1)

            def level_exp(g, n):
                act.wait_ge(l_sub, len(LEVELS) * g + n + 1)
                act.activation(temp(g, n), temp(g, n), ACT.Exp).then_inc(l_exp, 1)

            def context_exp(g):
                tt = tot[:, g % 2]
                act.wait_ge(gates, 2 * g + 2)
                for d in range(2):
                    lg, tc = heads(base(g) + (R_LF, R_LB)[d], N_LAT, NT), temp_lat(g, 1, d)
                    for h in range(HG):
                        for seg in range(2):
                            if d == 0:
                                bias = tt[:, d, h, 5:6] if seg == 0 else tt[:, d, h, 3:4]
                            else:
                                bias = 0.0 if seg == 0 else tt[:, d, h, 2:3]
                            m = act.activation(tc[:, h, seg * P:(seg + 1) * P], lg[:, h, seg * P:(seg + 1) * P],
                                               ACT.Exp, bias=bias, scale=-1.0 if d == 0 else 1.0)
                    m.then_inc(c_exp, 1)

            def cross_exp(g):
                act.wait_ge(st_mm, g + 1)
                for d in range(2):
                    m = act.activation(heads(base(g) + (R_LF, R_LB)[d], N_LAT, N_LAT + P),
                                       ps[:, 4, d * HG * P:(d + 1) * HG * P].rearrange("p (h c) -> p h c", h=HG), ACT.Copy)
                m.then_inc(st_cp, 1)
                tt, lf, lbk = tot[:, g % 2], heads(base(g) + R_LF, 0, N_LAT), heads(base(g) + R_LB, 0, N_LAT)
                keys, queries = temp_lat(g, 1, 0), temp_lat(g, 1, 1)
                for h in range(HG):
                    act.activation(keys[:, h, 0:P], lf[:, h, 0:P], ACT.Exp, bias=tt[:, 0, h, 0:1], scale=-1.0)
                    act.activation(queries[:, h, 0:P], lbk[:, h, 0:P], ACT.Exp, bias=tt[:, 1, h, 0:1], scale=-1.0)
                act.activation(keys[:, :, P:2 * P], lbk[:, :, P:2 * P], ACT.Exp)
                act.activation(queries[:, :, P:2 * P], lf[:, :, P:2 * P], ACT.Exp).then_inc(x_exp, 1)

            def initial_exp(g):
                act.wait_ge(l_mm, len(LEVELS) * g + 6)
                tt, lf, lbk = tot[:, g % 2], heads(base(g) + R_LF, 0, N_LAT), heads(base(g) + R_LB, 0, N_LAT)
                xf, xb = temp_lat(g, 1, 0), temp_lat(g, 1, 1)
                for h in range(HG):
                    act.activation(xf[:, h, P:2 * P], lf[:, h, P:2 * P], ACT.Exp, bias=tt[:, 0, h, 0:1])
                    act.activation(xb[:, h, 0:P], lbk[:, h, 0:P], ACT.Exp, bias=tt[:, 1, h, 4:5], scale=-1.0)
                    act.activation(xb[:, h, P:2 * P], lbk[:, h, P:2 * P], ACT.Exp, bias=tt[:, 1, h, 1:2], scale=-1.0)
                act.activation(xf[:, :, 0:P], lf[:, :, 0:P], ACT.Exp).then_inc(i_exp, 1)

            for g in range(-1, NG + 1):
                p, rec, end, proj = g + 1, 0 <= g < NG, g > 0, g < NG - 1
                for k in range(G_UNITS):
                    if k == 0 and rec:
                        context_exp(g)
                    if k == 0 and end:
                        initial_exp(g - 1)
                    if k == 1 and rec:
                        act.wait_ge(pe_used, U_IN_ODD + G_UNITS * (g + 1))
                        act.activation(ar(base(g) + R_Q, G_LAT), ps[:, 2, :], ACT.Silu).then_inc(q_rdy, 1)
                        act.activation(ar(base(g) + R_G, G_LAT), ps[:, 3, :], ACT.Silu).then_inc(g_rdy, 1)
                    if k == 2 and rec:
                        cross_exp(g)
                    if k == 2 and end:
                        act.wait_ge(o_cp, g)
                        act.activation(temp(g - 1, 1)[:, G_LAT:], temp(g - 1, 1)[:, 0:G_LAT], ACT.Square).then_inc(o_sq, 1)
                    if k == 3 and end:
                        std = temp(g - 1, 1)[:, G_LAT:]
                        act.wait_ge(o_var, g)
                        act.activation(std, std, ACT.Ln).then_inc(o_ln, 1)
                        act.wait_ge(o_ln, g)
                        act.activation(std, std, ACT.Exp, scale=-0.5).then_inc(o_std, 1)
                    if k >= 3 and rec:
                        level_exp(g, k - 3)
                    if k == 4 and end:
                        for h in range(HG):
                            n = (g - 1) * HG + h
                            act.wait_ge(r32_done, n + 1)
                            act.activation(s_hi[:, n * N_LAT:(n + 1) * N_LAT],
                                           temp_lat(g - 1, 1, 0)[:, h, :], ACT.Copy).then_inc(rhi_done, 1)
                    if k == 5 and proj:
                        gate_soft(p)
                    if k == 6 and proj:
                        act.wait_ge(pe_used, U_IN_ODD + G_UNITS * p + 6)
                        act.activation(ar(base(p) + R_V, TT * HG * P), ps[:, 0:2, :], ACT.Copy).then_inc(v_rdy, 1)
                    if k == 7 and proj:
                        gate_bound(p)
                    if k == 8 and proj:
                        for d in range(2):
                            gate_k(p, d)
                    split_to(units_before(g, k) + 1 + LEAD)
            split_to(U_OUT_ODD + 8 + LEAD)

            squares(3, N_LAT)
            norm_std(3, N_LAT)
            norm_hi(3, N_LAT)
            act.wait_ge(rt_in, 16)
            act.activation(rt_hi[:, :], rt32[:, :], ACT.Copy).then_inc(rt_hid, 1)
            act.wait_ge(rt_dif, 1)
            act.activation(route[:, :, 50:51], route[:, :, 50:51], ACT.Exp).then_inc(rt_exp, 1)
            n = 0
            for part in (s_hi, s_lo):
                for t in range(LT):
                    for kq in range(2):
                        act.wait_ge(tk_mm, n + 1)
                        act.activation(part[:, t * D + kq * BANK:t * D + (kq + 1) * BANK], ps[:, 4 + n % 4, :],
                                       ACT.Copy).then_inc(tk_out, 1)
                        n += 1
            act.wait_ge(routed, 1)
            n_turns = act.value_load(trips[0:1, 0:1], min_val=N_EXP, max_val=TURNS)

            def gather_hi(k):
                act.wait_ge(ga_mm, k)
                act.activation(s_hi[:, 2048:3072], ps[:, 0:2, :], ACT.Copy).then_inc(ga_hi, 1)

            def out_hi(i):
                act.wait_ge(ey32, i + 1)
                for half in range(2):
                    act.activation(y_parts(half)[0], ar(X_Y + half * BANK, BANK), ACT.Copy).then_inc(ey_hi, 1)

            gather_hi(1)
            with act.Fori(0, n_turns) as i:
                def turned_hi(cb):
                    act.wait_ge(et_mm, i * CB + (cb + 1))
                    act.activation(h_hi[:, cb * BANK:(cb + 1) * BANK], ps[:, 6, :], ACT.Copy).then_inc(et_hi, 1)

                for v in range(EXP_UNITS):
                    hi(U_MOE + LEAD + v, i, EXP_UNITS)
                    if v == 1:
                        out_hi(i)
                    if v % 8 == 0 and 8 <= v <= UP_UNITS:
                        act.wait_ge(pe_used, i * EXP_UNITS + (U_MOE + v))
                        act.activation(ar(X_SIL, BANK), ps[:, 2 * ((v // 8 - 1) % 2), :], ACT.Silu).then_inc(eu_silu, 1)
                    if v % 8 == 4 and 12 <= v <= UP_UNITS + 4:
                        turned_hi(v // 8 - 1)
                    if v == UP_UNITS + 12:
                        gather_hi(i + 2)
            out_hi(n_turns)

            for kt in range(KT):
                act.wait_ge(resid, 32 + kt + 1)
                act.wait_ge(sq_mm, KT * 4 + kt - 1)
                act.activation(ar(NORM_AT[4] + kt % 2 * NT, N_LAT), xT[:, kt, 0:N_LAT], ACT.Square).then_inc(sq_done, 1)
            norm_std(4, N_LAT)
            for n in range(4):
                act.wait_ge(fin_tr, n + 1)
                m = act.activation(ar(X_OUT + n * BANK, BANK), ps[:, 4 + n, :], ACT.Copy)
                if n % 2:
                    m.then_inc(fin_out, 1)

        @block.vector
        def _(dve):
            split = [0]
            seq = [0]

            def link(ins):
                seq[0] += 1
                ins.then_inc(dve_seq, 1)
                dve.wait_ge(dve_seq, seq[0])

            def lo(u, plus=0):
                dve.wait_ge(hi_done, plus + (u + 1))
                dve.tensor_tensor(w_lo[:, slot(u), :], raw[:, slot(u), :], w_hi[:, slot(u), :].bitcast(F32),
                                  ALU.subtract).then_inc(lo_done, 1)

            def split_to(n):
                while split[0] < n:
                    lo(split[0])
                    split[0] += 1

            def ada_cols(n, bank, layer, at, number):
                dve.wait_ge(ada_sel, number)
                src = ps[:, sel_bank(n, bank), 0:8].rearrange("p (q s) -> p q s", s=2)
                dve.tensor_tensor(adaT[:, layer, at, :], src, bias[:, layer, at, :], ALU.add).then_inc(ada_done, 1)

            def norm_var(n, width):
                inv = ar(NORM_AT[n] + 2 * NT, width)
                dve.wait_ge(sq_mm, KT * (n + 1))
                dve.tensor_scalar(inv, ps[:, 3, 0:width], 1.0 / D, EPS, ALU.mult, ALU.add).then_inc(var_done, 1)
                dve.wait_ge(std_done, n + 1)
                link(dve.reciprocal(inv, inv))

            def norm_dve(n, width, layer, gain, sh, sc, streams):
                base = NORM_AT[n]
                inv = ar(base + 2 * NT, width)
                for s in range(2):
                    m = dve.scalar_tensor_tensor(coef[:, :, s], adaT[:, layer, sc * KT:(sc + 1) * KT, s], 1.0,
                                                 vT[:, gain + layer * KT:gain + (layer + 1) * KT], ALU.add, ALU.mult)
                link(m)

                def lo_h(kt):
                    dve.wait_ge(hhi_done, KT * n + kt + 1)
                    dve.tensor_tensor(hl(kt, 0, width), ar(base + (3 + kt % 4) * NT, width),
                                      hh(kt, 0, width).bitcast(F32), ALU.subtract).then_inc(h_done, 1)

                for kt in range(KT):
                    if kt >= 2:
                        lo_h(kt - 2)
                    if kt >= 4:
                        dve.wait_ge(h_done, KT * n + kt - 3)
                    t = ar(base + (3 + kt % 4) * NT, width)
                    link(dve.tensor_tensor(t, xT[:, kt, 0:width], inv, ALU.mult))
                    for s in range(streams):
                        a, b = s * N_LAT, (s + 1) * N_LAT
                        m = dve.tensor_scalar(t[:, a:b], t[:, a:b], coef[:, kt, s:s + 1],
                                              adaT[:, layer, sh * KT + kt, s:s + 1], ALU.mult, ALU.add)
                    m.then_inc(h32_done, 1)
                lo_h(KT - 2)
                lo_h(KT - 1)

            def add_resid(kt, src, layer, gate, streams):
                for s in range(streams):
                    a, b = s * N_LAT, (s + 1) * N_LAT
                    m = dve.scalar_tensor_tensor(xT[:, kt, a:b], src[:, a:b],
                                                 adaT[:, layer, gate * KT + kt, s:s + 1], xT[:, kt, a:b],
                                                 ALU.mult, ALU.add)
                m.then_inc(resid, 1)

            dve.wait_ge(con_in, 16)
            dve.memset(cond[:, KT * 4:].bitcast(F32), 0.0).then_inc(vec_out, 1)
            dve.wait_ge(vec_tr, 1)
            dve.tensor_copy(vT[:, :], ps[:, 0, 0:V_ROWS])
            dve.tensor_copy(bT[:, :], ps[:, 0, 128:224]).then_inc(vec_out, 1)
            dve.wait_ge(vec_out, 2)
            bias = bT[:, :].rearrange("p (l v) -> p l v", l=2).unsqueeze(3).broadcast_to([P, 2, 48, 2])
            cv = cond[:, 0:KT * 4].rearrange("p (k s) -> p s k", s=4)
            for s in range(2):
                dve.wait_ge(cond_hi, 2)
                m = dve.tensor_tensor(cv[:, 2 + s, :], sil[:, s * KT:(s + 1) * KT], cv[:, s, :].bitcast(F32),
                                      ALU.subtract)
            m.then_inc(cond_rdy, 1)
            lbv = vT[:, V_LB:V_LB + 16]
            dve.tensor_tensor(lb[:, :], lbv, lbv, ALU.subtract).then_inc(lb_dif, 1)
            dve.wait_ge(lb_exp, 1)
            link(dve.reciprocal(lb1[:, :], lb[:, :]))
            link(dve.tensor_tensor(lb[:, :], lb[:, :], lb1[:, :], ALU.mult))
            link(dve.tensor_tensor(lb[:, :], lb[:, :], lb[:, :], ALU.subtract))
            link(dve.tensor_scalar(lb[:, :], lb[:, :], 0.0, 1.0, ALU.max, ALU.min))
            link(dve.tensor_scalar(lb1[:, :], lb[:, :], -1.0, 1.0, ALU.mult, ALU.add))

            split_to(R - 1)
            norm_var(0, NT)
            for n in range(4):
                split_to(4 * n + 4 + LEAD)
                ada_cols(n, 0, 0, slice(4 * n, 4 * n + 4), n + 1)
            dve.wait_ge(ada_done, 4)
            norm_dve(0, NT, 0, V_NMIX, SH_M, SC_M, 2)

            split_to(U_IN_EVEN + 4 + LEAD)
            dve.wait_ge(pe_used, U_IN_EVEN + 4)
            for n in range(4):
                dve.tensor_copy(ar(M_A + n * NT, NT), ps[:, n, :]).then_inc(a_out, 1)
            split_to(U_IN_EVEN + 12 + LEAD)
            for t in range(TT):
                dve.wait_ge(v_out, t + 1)
                for h in range(B_H):
                    m = dve.bn_stats(stats[:, t * B_H + h, :], ar(M_V + t * BANK + h * P, P))
            link(m)
            for k in range(16):
                m = dve.bn_aggr(mv[:, k, :], stats[:, k, :])
            link(m)
            dve.tensor_scalar(rs[:, :], mv[:, :, 1], EPS, None, ALU.add).then_inc(lnv, 1)
            for n in range(4, 6):
                split_to(U_ADA_C + 4 * (n - 3) + LEAD)
                ada_cols(n, 4, 0, slice(4 * n, 4 * n + 4), n + 1)
            dve.wait_ge(lns, 1)
            link(dve.reciprocal(rs[:, :], rs[:, :]))
            for k in range(16):
                vt = ar(M_V + k * P, P)
                dve.tensor_scalar(vt, vt, mv[:, k, 0:1], rs[:, k:k + 1], ALU.subtract, ALU.mult).then_inc(ln_done, 1)
            for g in range(4):
                dve.wait_ge(yhi_done, g + 1)
                dve.tensor_tensor(hl(g), ps[:, g, :], hh(g).bitcast(F32), ALU.subtract).then_inc(ylo_done, 1)
            for h in range(4):
                dve.wait_ge(y_mm, 4 + h + 1)
                if h >= 2:
                    dve.wait_ge(ylo_done, 4 + h - 1)
                dve.tensor_tensor(ar(M_TMP + h % 2 * NT, NT), ps[:, 4 + h, :], ar(M_U + h * NT, NT),
                                  ALU.mult).then_inc(y32_done, 1)
                dve.wait_ge(yhi_done, 4 + h + 1)
                dve.tensor_tensor(hl(4 + h), ar(M_TMP + h % 2 * NT, NT), hh(4 + h).bitcast(F32),
                                  ALU.subtract).then_inc(ylo_done, 1)
            for blk in range(2):
                split_to(U_OUT_EVEN + 4 * blk + 4 + LEAD)
                dve.wait_ge(pe_used, U_OUT_EVEN + 4 * (blk + 1))
                for n in range(4):
                    add_resid(4 * blk + n, ps[:, 4 * blk + n, :], 0, G_M, 2)
            norm_var(1, NT)
            with dve.Fori(0, 2) as j:
                for n in range(3):
                    for k in range(4):
                        lo(U_ADA_E + LEAD + 4 * n + k, plus=j * 12)
                    ada_cols(n, 0, 0, bass.ds(j * 12 + (24 + 4 * n), 4), j * 3 + (7 + n))
            split[0] = U_FFN + LEAD
            dve.wait_ge(ada_done, 12)
            norm_dve(1, NT, 0, V_NFFN, SH_F, SC_F, 2)
            def hidden_lo(f, tile):
                dve.wait_ge(hidhi, tile + 1)
                sl = slice(f % 6 * NT, (f % 6 + 1) * NT)
                dve.tensor_tensor(s_lo[:, sl], ar(F_HID + f * NT, NT), s_hi[:, sl].bitcast(F32),
                                  ALU.subtract).then_inc(hidlo, 1)

            u = U_FFN
            for half, (first, count) in enumerate(FF_HALF):
                for it in range(first, first + count):
                    if it == first + count - 1:
                        for f in range(4):
                            hidden_lo(f, 2 * first + f)
                    u += 4
                    split_to(u + LEAD)
                    dve.wait_ge(up_silu, it + 1)
                    f = it - first
                    dve.tensor_tensor(ar(F_HID + f * 1024, 1024).rearrange("p (b t) -> p b t", b=2),
                                      ps[:, 4 * (it % 2) + 2:4 * (it % 2) + 4, :],
                                      ar(F_SIL + it % 2 * 1024, 1024).rearrange("p (b t) -> p b t", b=2),
                                      ALU.mult).then_inc(hid_done, 1)
                for f in range(2 * count):
                    if f >= 4:
                        hidden_lo(f, 2 * first + f)
                    split_to(u + f + LEAD)
                u += 2 * count
                split_to(u + LEAD)
                dve.wait_ge(pe_used, u)
                for n in range(KT):
                    add_resid(n, ps[:, n, :], 0, G_F, 2)
            norm_var(2, NT)
            with dve.Fori(0, 4) as j:
                for n in range(3):
                    for k in range(4):
                        lo(U_ADA_G + LEAD + 4 * n + k, plus=j * 12)
                    ada_cols(n, 0, 1, bass.ds(j * 12 + 4 * n, 4), j * 3 + (13 + n))
            split[0] = U_IN_ODD + LEAD
            dve.wait_ge(ada_done, 24)
            norm_dve(2, NT, 1, V_NMIX, SH_M, SC_M, 2)

            def gate_out(p, d):
                dve.wait_ge(pe_used, U_IN_ODD + G_UNITS * p + 2 * d + 2)
                if d == 0 and p >= 2:
                    dve.wait_ge(o_mm, p - 1)
                if d == 1 and p > 0:
                    dve.wait_ge(gates, 2 * p)
                if d == 0 and p >= 2:
                    dve.wait_ge(rlo_done, (p - 1) * HG)
                z = ar(base(p) + (R_LF, R_LB)[d], HG * NT)
                dve.tensor_scalar(z.rearrange("p (h t) -> p h t", h=HG), ps[:, 2 * d:2 * d + 2, :], LN_FLOOR, None,
                                  ALU.max).then_inc(z_out, 1)
                dve.wait_ge(z_out, 2 * p + d + 1)
                dve.scalar_tensor_tensor(gate_temp(p, d), z, -1.0, z, ALU.mult, ALU.min).then_inc(z_abs, 1)

            def gate_logs(p, d):
                dve.wait_ge(soft_rdy, 2 * p + d + 1)
                kfl, lfl = (ar(base(p) + a[d], HG * NT) for a in ((R_KF, R_KB), (R_LF, R_LB)))
                dve.scalar_tensor_tensor(kfl, lfl, 0.0, gate_temp(p, d), ALU.max, ALU.add).then_inc(soft_out, 1)
                dve.wait_ge(soft_out, 2 * p + d + 1)
                dve.scalar_tensor_tensor(lfl, lfl, 0.0, gate_temp(p, d), ALU.min, ALU.subtract).then_inc(s_log, 1)
                dve.wait_ge(s_log, 2 * p + d + 1)
                dve.tensor_scalar(gate_temp(p, d), lfl, -LN_MAX, None, ALU.max).then_inc(s_cut, 1)

            def gate_scale(p, d):
                dve.wait_ge(k_exp, 2 * p + d + 1)
                for h in range(HG):
                    col = d * HEADS + p * HG + h
                    kh = heads(base(p) + (R_KF, R_KB)[d])[:, h, :]
                    m = dve.tensor_scalar(kh, kh, lb1[:, col:col + 1], None, ALU.mult)
                m.then_inc(k_rdy, 1)

            def gate_sums(p, d):
                if d == 0:
                    dve.wait_ge(ln_rdy, 2 * p + 1)
                else:
                    dve.wait_ge(l_add, p + 1)
                lfl, tfl = ar(base(p) + (R_LF, R_LB)[d], HG * NT), gate_temp(p, d)
                tt = tot[:, p % 2, d]
                l4 = lfl.rearrange("p (h s t) -> p h s t", h=HG, s=TT)
                t4 = tfl.rearrange("p (h s t) -> p h s t", h=HG, s=TT)
                for s in range(HG * TT):
                    a = s * P
                    if d == 0:
                        m = dve.tensor_tensor_scan(lfl[:, a:a + P], lfl[:, a:a + P], tfl[:, a:a + P], 0.0, ALU.add, ALU.add)
                    else:
                        m = dve.tensor_tensor_scan(lfl[:, a + 1:a + P], ones[:, 0:P - 1], tfl[:, a:a + P - 1], 0.0,
                                                   ALU.mult, ALU.add)
                if d == 1:
                    m = dve.memset(l4[:, :, :, 0:1], 0.0)
                link(m)
                if d == 0:
                    link(dve.tensor_copy(tt[:, :, 0:4], l4[:, :, :, P - 1]))
                else:
                    link(dve.tensor_tensor(tt[:, :, 0:4], l4[:, :, :, P - 1], t4[:, :, :, P - 1], ALU.add))
                for k in range(2):
                    m = dve.tensor_tensor(tt[:, :, 4 + k:5 + k], tt[:, :, 2 * k:2 * k + 1],
                                          tt[:, :, 2 * k + 1:2 * k + 2], ALU.add)
                m.then_inc(gates, 1)

            def blocks(view, hs):
                return view.rearrange("p h (b c) -> p h b c", c=2 * hs)

            def level_mul(g, n):
                dve.wait_ge(l_exp, len(LEVELS) * g + n + 1)
                hs = LEVELS[n]
                keys = blocks(temp_lat(g, n, 0), hs)
                kf, kb = (blocks(heads(base(g) + a, 0, N_LAT), hs) for a in (R_KF, R_KB))
                dve.tensor_tensor(keys[:, :, :, 0:hs], keys[:, :, :, 0:hs], kf[:, :, :, 0:hs], ALU.mult)
                dve.tensor_tensor(keys[:, :, :, hs:], keys[:, :, :, hs:], kb[:, :, :, hs:], ALU.mult)
                queries = temp(g, n)[:, G_LAT:]
                dve.tensor_tensor(queries, queries, ar(base(g) + R_Q, G_LAT), ALU.mult).then_inc(l_mul, 1)

            def masked(g, n):
                dve.wait_ge(l_mm, len(LEVELS) * g + n + 1)
                if n == 0:
                    dve.wait_ge(mask_rdy, 1)
                    dve.wait_ge(dg_out, g + 1)
                else:
                    dve.wait_ge(l_cp, len(LEVELS) * g + n)
                mk = masks[:, n * P:(n + 1) * P].unsqueeze(1).unsqueeze(1).broadcast_to([P, 2, HG, P])
                dve.copy_predicated(scores(g), mk, by_half(6 - n % 2)).then_inc(l_cp, 1)

            for g in range(-1, NG + 1):
                p, rec, end, proj = g + 1, 0 <= g < NG, g > 0, g < NG - 1
                o32, std = temp(g - 1, 1)[:, 0:G_LAT], temp(g - 1, 1)[:, G_LAT:]
                for k in range(G_UNITS):
                    if k == 0 and end:
                        level_mul(g - 1, 6)
                        masked(g - 1, 5)
                    if k == 0 and rec:
                        dve.wait_ge(k_rdy, 2 * g + 2)
                        for d in range(2):
                            dve.wait_ge(c_exp, 2 * g + d + 1)
                            kb = heads(base(g) + (R_KF, R_KB)[d], N_LAT, NT)
                            dve.tensor_tensor(kb, kb, temp_lat(g, 1, d), ALU.mult).then_inc(c_mul, 1)
                    if k == 1 and end:
                        masked(g - 1, 6)
                        dve.wait_ge(i_exp, g)
                        both = temp(g - 1, 1).rearrange("p (d t) -> p d t", d=2)
                        q2 = ar(base(g - 1) + R_Q, G_LAT).unsqueeze(1).broadcast_to([P, 2, G_LAT])
                        dve.tensor_tensor(both, both, q2, ALU.mult).then_inc(i_mul, 1)
                    if k == 1 and rec:
                        for d in range(2):
                            dve.wait_ge(c_tr, 2 * g + d + 1)
                            dve.wait_ge(c_mul, 2 * g + 2)
                            dve.tensor_copy(temp(g, 1)[:, d * BANK:(d + 1) * BANK], ps[:, 4 + d, :]).then_inc(c_cp, 1)
                    if k == 2 and end:
                        dve.wait_ge(o_mm, g)
                        dve.tensor_scalar(o32, ps[:, 7, :], P ** -0.5, None, ALU.mult).then_inc(o_cp, 1)
                    if k == 2 and rec:
                        dve.wait_ge(x_exp, g + 1)
                        dve.wait_ge(q_rdy, g + 1)
                        keys, queries = temp_lat(g, 1, 0), temp(g, 1)[:, G_LAT:]
                        for d in range(2):
                            a = slice(d * P, (d + 1) * P)
                            kk = heads(base(g) + (R_KF, R_KB)[d], 0, N_LAT)
                            dve.tensor_tensor(keys[:, :, a], keys[:, :, a], kk[:, :, a], ALU.mult)
                        dve.tensor_tensor(queries, queries, ar(base(g) + R_Q, G_LAT), ALU.mult).then_inc(x_mul, 1)
                    if k == 3 and end:
                        dve.wait_ge(o_sum, g)
                        dve.tensor_scalar(std, ps[:, 6, :], 1.0 / P, EPS, ALU.mult, ALU.add).then_inc(o_var, 1)
                    if k == 3 and rec:
                        dve.wait_ge(dg_mm, g + 1)
                        id4 = ident.unsqueeze(1).unsqueeze(1).broadcast_to([P, 2, HG, P])
                        dve.tensor_tensor(scores(g), by_half(5), id4, ALU.mult).then_inc(dg_out, 1)
                    if k >= 4 and rec:
                        level_mul(g, k - 4)
                    if k == 4 and rec:
                        dve.wait_ge(x_mm, g + 1)
                        for d in range(2):
                            m = dve.tensor_copy(heads(base(g) + (R_KF, R_KB)[d], N_LAT, NT)[:, :, (1 - d) * P:(2 - d) * P],
                                                ps[:, 4, d * HG * P:(d + 1) * HG * P].rearrange("p (h t) -> p h t", h=HG))
                        m.then_inc(x_cp, 1)
                    if k == 4 and end:
                        dve.wait_ge(o_std, g)
                        link(dve.tensor_tensor(o32, o32, std, ALU.mult))
                        for h in range(HG):
                            col = V_RNORM + (g - 1) * HG + h
                            oh = temp_lat(g - 1, 1, 0)[:, h, :]
                            dve.scalar_tensor_tensor(oh, oh, vT[:, col:col + 1], lat(base(g - 1) + R_G)[:, h, :],
                                                     ALU.mult, ALU.mult).then_inc(r32_done, 1)
                    if k == 4 and end:
                        for h in range(HG):
                            n = (g - 1) * HG + h
                            dve.wait_ge(rhi_done, n + 1)
                            dve.tensor_tensor(s_lo[:, n * N_LAT:(n + 1) * N_LAT], temp_lat(g - 1, 1, 0)[:, h, :],
                                              s_hi[:, n * N_LAT:(n + 1) * N_LAT].bitcast(F32),
                                              ALU.subtract).then_inc(rlo_done, 1)
                    if k == 4 and proj:
                        for d in range(2):
                            gate_out(p, d)
                    if k >= 5 and rec:
                        masked(g, k - 5)
                    if k == 6 and proj:
                        for d in range(2):
                            gate_logs(p, d)
                    if k == 8 and proj:
                        gate_sums(p, 0)
                    if k == 9 and proj:
                        gate_sums(p, 1)
                        for d in range(2):
                            gate_scale(p, d)
                    split_to(units_before(g, k) + 1 + LEAD)
            split_to(U_OUT_ODD + 8 + LEAD)
            for blk in range(2):
                dve.wait_ge(pe_used, U_OUT_ODD + 7 + blk)
                for n in range(4):
                    add_resid(4 * blk + n, ps[:, 2 * blk + n // 2, n % 2 * 256:n % 2 * 256 + 256], 1, G_M, 1)
            norm_var(3, N_LAT)
            norm_dve(3, N_LAT, 1, V_NFFN, SH_F, SC_F, 1)

            dve.wait_ge(rt_hid, 1)
            dve.tensor_tensor(rt_lo[:, :], rt32[:, :], rt_hi[:, :].bitcast(F32), ALU.subtract).then_inc(rt_rdy, 1)
            dve.wait_ge(lg_mm, 1)
            for t in range(LT):
                m = dve.tensor_copy(route[:, t, 0:8], ps[:, 2 * t, 0:N_EXP])
            link(m)
            for t in range(LT):
                m = dve.max(route[:, t, 8:16], route[:, t, 0:8])
            link(m)
            for t in range(LT):
                m = dve.max_index(idx[:, t, :], route[:, t, 8:16], route[:, t, 0:8])
            link(m)
            link(dve.tensor_copy(route[:, :, 16:18], idx[:, :, 0:2]))
            dve.tensor_tensor(route[:, :, 50:51], route[:, :, 9:10], route[:, :, 8:9], ALU.subtract).then_inc(rt_dif, 1)
            for t in range(LT):
                for k in range(2):
                    at = (18, 40)[k]
                    m = dve.tensor_scalar(route[:, t, at:at + 8], iota[:, 0:8], route[:, t, 16 + k:17 + k], None,
                                          ALU.is_equal)
            link(m)
            dve.tensor_tensor(route[:, :, 32:40], route[:, :, 18:26], route[:, :, 40:48], ALU.add).then_inc(pick, 1)
            dve.wait_ge(pick, 1)
            dve.wait_ge(rt_exp, 1)
            link(dve.tensor_scalar(route[:, :, 51:52], route[:, :, 50:51], 1.0, None, ALU.add))
            link(dve.reciprocal(route[:, :, 51:52], route[:, :, 51:52]))
            link(dve.tensor_tensor(route[:, :, 52:53], route[:, :, 50:51], route[:, :, 51:52], ALU.mult))
            for t in range(LT):
                m = dve.tensor_scalar(route[:, t, 18:26], route[:, t, 18:26], route[:, t, 51:52], None, ALU.mult)
            link(m)
            for t in range(LT):
                m = dve.scalar_tensor_tensor(comb[:, t, 0:N_EXP], route[:, t, 40:48], route[:, t, 52:53],
                                             route[:, t, 18:26], ALU.mult, ALU.add)
            dve.wait_ge(rk_mm, 1)
            link(dve.tensor_scalar(route[:, :, 53:61], route[:, :, 32:40], -1024.0, 1024.0, ALU.mult, ALU.add))
            link(dve.tensor_tensor(rank[:, :, 0:8], ps[:, 1, 0:16].rearrange("p (t e) -> p t e", e=8),
                                   route[:, :, 53:61], ALU.add))
            dve.memset(rank[:, :, TURNS:], 1024.0)
            dve.memset(comb[:, :, TURNS:], 0.0)
            sel, order = over[:, O_SEL:O_SEL + N_EXP], over[:, O_ORDER:O_ORDER + N_EXP]
            link(dve.tensor_scalar(sel, ps[:, 1, 16:24], float(SLOTS), None, ALU.is_gt))
            link(dve.tensor_tensor_scan(order, ones[:, 0:N_EXP], sel, 0.0, ALU.mult, ALU.add))
            dve.tensor_copy(cnt[:, T_OVER:T_OVER + 1], order[:, N_EXP - 1:N_EXP])
            link(dve.tensor_scalar(cnt[:, T_TURNS:T_TURNS + 1], order[:, N_EXP - 1:N_EXP], float(N_EXP), None, ALU.add))
            pick_over = over[:, O_PICK:O_PICK + N_OVER * N_EXP].rearrange("p (j e) -> p j e", e=N_EXP)
            for j in range(N_OVER):
                m = dve.scalar_tensor_tensor(pick_over[:, j, :], order, float(j + 1), sel, ALU.is_equal, ALU.mult)
            link(m)
            tmp = over[:, O_TMP:].rearrange("p (t j e) -> p t j e", t=LT, e=N_EXP)
            link(dve.tensor_tensor(tmp[:, 0], pick_over, iota[:, 0:N_EXP].unsqueeze(1).broadcast_to([P, N_OVER, N_EXP]),
                                   ALU.mult))
            link(dve.tensor_reduce(cnt[:, T_EXPERT:].unsqueeze(2), tmp[:, 0], AX.X, ALU.add))
            for full in (rank, comb):
                for t in range(LT):
                    m = dve.tensor_tensor(tmp[:, t], pick_over,
                                          full[:, t, 0:N_EXP].unsqueeze(1).broadcast_to([P, N_OVER, N_EXP]), ALU.mult)
                link(m)
                for t in range(LT):
                    m = dve.tensor_reduce(full[:, t, N_EXP:TURNS].unsqueeze(2), tmp[:, t], AX.X, ALU.add)
                link(m)
            link(dve.tensor_scalar(rank[:, :, N_EXP:TURNS], rank[:, :, N_EXP:TURNS], -float(SLOTS), None, ALU.add))
            link(dve.tensor_copy(trips[:, :], cnt[:, :]))
            dve.memset(spread[:, :].bitcast(F32), 0.0).then_inc(sp_rdy, 1)
            dve.memset(cslot[:, :], 0.0).then_inc(routed, 1)
            dve.wait_ge(routed, 1)

            def gather_lo(k):
                dve.wait_ge(ga_hi, k)
                dve.tensor_copy(s_lo[:, 2048:3072], ps[:, 2:4, :]).then_inc(ga_lo, 1)

            def one_hots(i):
                for t in range(LT):
                    dve.tensor_scalar(onehot[:, t, :], iota, rank[:, t, bass.ds(i, 1)] if not isinstance(i, int)
                                      else rank[:, t, i:i + 1], None, ALU.is_equal)
                src = comb[:, :, bass.ds(i, 1)] if not isinstance(i, int) else comb[:, :, i:i + 1]
                dve.tensor_copy(cw[:, :].unsqueeze(2), src).then_inc(oh_rdy, 1)

            one_hots(0)
            gather_lo(1)
            n_turns = dve.value_load(trips[0:1, 0:1], min_val=N_EXP, max_val=TURNS)
            acc = ar(X_ACC, KT * N_LAT)

            def out_scale(i):
                dve.wait_ge(pe_used, i * EXP_UNITS + U_MOE)
                dve.wait_ge(sp_rdy, i + 1)
                dve.tensor_scalar(ar(X_Y, D).rearrange("p (b t) -> p b t", b=2), ps[:, 4:6, :], cslot[:, 0:1], None,
                                  ALU.mult).then_inc(ey32, 1)

            def out_lo(i, half):
                yh, yl = y_parts(half)
                dve.wait_ge(ey_hi, i * 2 + (half + 1))
                dve.tensor_tensor(yl, ar(X_Y + half * BANK, BANK), yh.bitcast(F32), ALU.subtract).then_inc(ey_lo, 1)

            def out_add(i, half):
                dve.wait_ge(sc_mm, i * 2 + (half + 1))
                dve.wait_ge(acc_rdy, i * 2 + (half + 1))
                a = acc[:, half * 1024:(half + 1) * 1024].rearrange("p (b t) -> p b t", b=2)
                dve.tensor_tensor(a, a, ps[:, 6:8, :], ALU.add).then_inc(acc_rdy, 1)

            with dve.Fori(0, n_turns) as i:
                past = i * EXP_UNITS

                def turned_lo(cb):
                    dve.wait_ge(et_hi, i * CB + (cb + 1))
                    dve.tensor_tensor(h_lo[:, cb * BANK:(cb + 1) * BANK], ps[:, 6, :],
                                      h_hi[:, cb * BANK:(cb + 1) * BANK].bitcast(F32), ALU.subtract).then_inc(et_lo, 1)

                for v in range(EXP_UNITS):
                    lo(U_MOE + LEAD + v, plus=past)
                    if v == 0:
                        out_scale(i)
                    if v in (1, 2):
                        out_lo(i, v - 1)
                    if v in (5, 7):
                        out_add(i, (v - 5) // 2)
                    if v % 8 == 0 and 8 <= v <= UP_UNITS:
                        dve.wait_ge(eu_silu, i * CB + (v // 8))
                        dve.tensor_tensor(ar(X_HID, BANK), ps[:, 2 * ((v // 8 - 1) % 2) + 1, :], ar(X_SIL, BANK),
                                          ALU.mult).then_inc(eu_hid, 1)
                    if v % 8 == 4 and 12 <= v <= UP_UNITS + 4:
                        turned_lo(v // 8 - 1)
                    if v == 25:
                        dve.wait_ge(sp_mm, i + 1)
                        dve.tensor_copy(spread[:, :], ps[:, 7, 0:256])
                        dve.tensor_copy(cslot[:, :], ps[:, 7, 256:257]).then_inc(sp_rdy, 1)
                    if v == UP_UNITS + 5:
                        one_hots(i + 1)
                    if v == UP_UNITS + 12:
                        gather_lo(i + 2)
            out_scale(n_turns)
            for half in range(2):
                out_lo(n_turns, half)
            for half in range(2):
                out_add(n_turns, half)

            dve.wait_ge(acc_rdy, n_turns * 2 + 3)
            for n in range(KT):
                add_resid(n, acc[:, n * N_LAT:(n + 1) * N_LAT], 1, G_F, 1)
            dve.wait_ge(sq_mm, KT * 5)
            inv = ar(NORM_AT[4] + 2 * NT, N_LAT)
            dve.tensor_scalar(inv, ps[:, 3, 0:N_LAT], 1.0 / D, EPS, ALU.mult, ALU.add).then_inc(var_done, 1)
            dve.wait_ge(std_done, 5)
            link(dve.reciprocal(inv, inv))
            for kt in range(KT):
                dve.scalar_tensor_tensor(xT[:, kt, 0:N_LAT], xT[:, kt, 0:N_LAT], vT[:, V_NOUT + kt:V_NOUT + kt + 1], inv,
                                         ALU.mult, ALU.mult).then_inc(fin32, 1)


_INS = ["x", "c", "ctx", "c_ctx", "w_ada", "b_ada", "norm_mix", "norm_ffn", "norm_out", "w_in_even", "gmlp_w",
        "gmlp_b", "w_out_even", "w_in_odd", "rec_lb", "rec_norm", "w_out_odd", "ffn_w1", "ffn_w3", "ffn_w2",
        "router_w", "moe_w1", "moe_w3", "moe_w2"]


def kernel(**inputs):
    import concourse.bacc as _bacc
    from concourse.bass_utils import run_bass_kernel_spmd as _run

    nc = _bacc.Bacc("TRN2", target_bir_lowering=False, num_devices=1, dynamic_dma_scratch_size=1024)
    arrays, args = {}, []
    for name in _INS:
        a = np.asarray(inputs[name])
        if name == "gmlp_w":
            a = a[0].transpose(2, 0, 1)
        a = np.ascontiguousarray(a)
        arrays[f"in_{name}"] = a
        args.append(nc.dram_tensor(f"in_{name}", a.shape, mybir.dt.from_np(a.dtype), kind="ExternalInput").ap())
    for name, a in zip(("cst", "msk"), constants()):
        arrays[name] = a
        args.append(nc.dram_tensor(name, a.shape, mybir.dt.from_np(a.dtype), kind="ExternalInput").ap())
    args.append(nc.dram_tensor("out", (1, N_LAT, D), F32, kind="ExternalOutput").ap())
    build(nc, *args)
    return _run(nc, [arrays], core_ids=[0]).results[0]["out"]
```
